# Optimizing a Trainium2 kernel written in Bass

```python
import math
import jax, jax.numpy as jnp
from jax import lax
import numpy as np

D_MODEL = 1024
BATCH = 1
SEQ = 512
DEPTH = 1

N_META = 16
HEAD_DIM = 64
SWA_Q_HEADS = D_MODEL // (2 * HEAD_DIM)
SWA_KV_HEADS = max(SWA_Q_HEADS // 4, 1)
SWA_GROUP = SWA_Q_HEADS // SWA_KV_HEADS
FOX_HEADS = D_MODEL // (2 * HEAD_DIM)
SWA_Q_W = SWA_Q_HEADS * HEAD_DIM
SWA_KV_W = SWA_KV_HEADS * HEAD_DIM
FOX_W = FOX_HEADS * HEAD_DIM
D_MIX = SWA_Q_W + FOX_W
OFF_QA = SWA_Q_W
OFF_KA = OFF_QA + SWA_KV_W
OFF_VA = OFF_KA + SWA_KV_W
OFF_QB = OFF_VA + FOX_W
OFF_KB = OFF_QB + FOX_W
OFF_VB = OFF_KB + FOX_W
D_PROJ = OFF_VB + FOX_HEADS
WINDOW = 128
BLOCK = 128
N_BUCKETS = 32
MAX_DISTANCE = 128
D_FF = -(-8 * D_MODEL // (3 * 256)) * 256
EPS = 1e-6
NEG_INF = -1e30


def rms_norm(x, g):
    xf = x.astype(jnp.float32)
    y = xf * lax.rsqrt(jnp.mean(xf * xf, axis=-1, keepdims=True) + EPS)
    return (y * g.astype(jnp.float32)).astype(x.dtype)

def t5_bucket(dist):
    n = jnp.maximum(dist, 0).astype(jnp.int32)
    max_exact = N_BUCKETS // 2
    nf = jnp.maximum(n, 1).astype(jnp.float32)
    large = max_exact + (jnp.log(nf / max_exact) / math.log(MAX_DISTANCE / max_exact)
                         * (N_BUCKETS - max_exact)).astype(jnp.int32)
    large = jnp.minimum(large, N_BUCKETS - 1)
    return jnp.where(n < max_exact, n, large)

def softmax_with_sink(s, sink):
    sink_r = sink.reshape((1,) + sink.shape + (1,) * (s.ndim - 3))
    col = jnp.broadcast_to(sink_r, s.shape[:-1] + (1,))
    p = jax.nn.softmax(jnp.concatenate([s, col], axis=-1), axis=-1)
    return p[..., :-1]

def swa_sink_attention(q, k, v, sinks, rel_bias):
    B, L = q.shape[0], q.shape[1]
    n_blk = (L - N_META) // BLOCK
    scale = HEAD_DIM ** -0.5
    sink = sinks.astype(jnp.float32).reshape(SWA_KV_HEADS, SWA_GROUP)
    tab = rel_bias.astype(jnp.float32)
    mi = jnp.arange(N_META)
    km, vm = k[:, :N_META], v[:, :N_META]

    qm = q[:, :N_META].reshape(B, N_META, SWA_KV_HEADS, SWA_GROUP, HEAD_DIM)
    d_mm = mi[:, None] - mi[None, :]
    b_mm = tab[t5_bucket(d_mm)].transpose(2, 0, 1).reshape(SWA_KV_HEADS, SWA_GROUP, N_META, N_META)
    s_mm = jnp.einsum('bqhgd,bkhd->bhgqk', qm, km, preferred_element_type=jnp.float32) * scale + b_mm
    s_mm = jnp.where(d_mm >= 0, s_mm, NEG_INF)
    p_mm = softmax_with_sink(s_mm, sink).astype(v.dtype)
    o_meta = jnp.einsum('bhgqk,bkhd->bqhgd', p_mm, vm).reshape(B, N_META, SWA_Q_HEADS, HEAD_DIM)

    qr = q[:, N_META:].reshape(B, n_blk, BLOCK, SWA_KV_HEADS, SWA_GROUP, HEAD_DIM)
    kr = k[:, N_META:].reshape(B, n_blk, BLOCK, SWA_KV_HEADS, HEAD_DIM)
    vr = v[:, N_META:].reshape(B, n_blk, BLOCK, SWA_KV_HEADS, HEAD_DIM)

    def with_prev(t):
        prev = jnp.pad(t, ((0, 0), (1, 0), (0, 0), (0, 0), (0, 0)))[:, :-1]
        return jnp.concatenate([prev, t], axis=2)

    kw, vw = with_prev(kr), with_prev(vr)
    qi = jnp.arange(BLOCK)[:, None]
    ki = jnp.arange(2 * BLOCK)[None, :]
    d_w = qi + BLOCK - ki
    b_w = tab[t5_bucket(d_w)].transpose(2, 0, 1).reshape(SWA_KV_HEADS, SWA_GROUP, 1, BLOCK, 2 * BLOCK)
    blk = jnp.arange(n_blk)[:, None, None]
    valid_w = ((d_w >= 0) & (d_w < WINDOW))[None] & ((blk > 0) | (ki >= BLOCK)[None])
    s_w = jnp.einsum('bnqhgd,bnkhd->bhgnqk', qr, kw, preferred_element_type=jnp.float32) * scale + b_w
    s_w = jnp.where(valid_w, s_w, NEG_INF)
    d_m = N_META + blk * BLOCK + qi[None] - mi[None, None, :]
    b_m = tab[t5_bucket(d_m)].transpose(3, 0, 1, 2).reshape(SWA_KV_HEADS, SWA_GROUP, n_blk, BLOCK, N_META)
    s_m = jnp.einsum('bnqhgd,bmhd->bhgnqm', qr, km, preferred_element_type=jnp.float32) * scale + b_m
    p = softmax_with_sink(jnp.concatenate([s_m, s_w], axis=-1), sink).astype(v.dtype)
    o = (jnp.einsum('bhgnqm,bmhd->bnqhgd', p[..., :N_META], vm)
         + jnp.einsum('bhgnqk,bnkhd->bnqhgd', p[..., N_META:], vw))
    o_real = o.reshape(B, n_blk * BLOCK, SWA_Q_HEADS, HEAD_DIM)
    return jnp.concatenate([o_meta, o_real], axis=1)

def forgetting_attention(q, k, v, f_logit):
    B, L = q.shape[0], q.shape[1]
    n_blk = (L - N_META) // BLOCK
    scale = HEAD_DIM ** -0.5
    cum = jnp.cumsum(jax.nn.log_sigmoid(f_logit.astype(jnp.float32)), axis=1).transpose(0, 2, 1)

    mi = jnp.arange(N_META)
    s = jnp.einsum('bqhd,bkhd->bhqk', q[:, :N_META], k[:, :N_META], preferred_element_type=jnp.float32) * scale
    s = s + cum[:, :, :N_META, None] - cum[:, :, None, :N_META]
    s = jnp.where(mi[:, None] >= mi[None, :], s, NEG_INF)
    p = jax.nn.softmax(s, axis=-1).astype(v.dtype)
    o_meta = jnp.einsum('bhqk,bkhd->bqhd', p, v[:, :N_META])

    qb = q[:, N_META:].reshape(B, n_blk, BLOCK, FOX_HEADS, HEAD_DIM).transpose(1, 0, 2, 3, 4)
    cb = cum[:, :, N_META:].reshape(B, FOX_HEADS, n_blk, BLOCK).transpose(2, 0, 1, 3)
    k_pos = jnp.arange(L)

    def one_block(args):
        q_blk, c_blk, b = args
        q_pos = N_META + b * BLOCK + jnp.arange(BLOCK)
        sb = jnp.einsum('bqhd,bkhd->bhqk', q_blk, k, preferred_element_type=jnp.float32) * scale
        sb = sb + c_blk[..., None] - cum[:, :, None, :]
        sb = jnp.where(k_pos[None, :] <= q_pos[:, None], sb, NEG_INF)
        pb = jax.nn.softmax(sb, axis=-1).astype(v.dtype)
        return jnp.einsum('bhqk,bkhd->bqhd', pb, v)

    o = lax.map(one_block, (qb, cb, jnp.arange(n_blk)))
    o_real = o.transpose(1, 0, 2, 3, 4).reshape(B, n_blk * BLOCK, FOX_HEADS, HEAD_DIM)
    return jnp.concatenate([o_meta, o_real], axis=1)

def first_inputs(seed: int = 0) -> dict:
    key = jax.random.key(seed)
    ks = jax.random.split(key, 14)
    f32 = jnp.float32
    gain = lambda k: 1.0 + 0.05 * jax.random.normal(k, (DEPTH, D_MODEL), f32)
    return {
        "x": jax.random.normal(ks[0], (BATCH, SEQ, D_MODEL), f32),
        "meta_tokens": jax.random.normal(ks[1], (N_META, D_MODEL), f32),
        "rel_bias": 0.5 * jax.random.normal(ks[2], (N_BUCKETS, SWA_Q_HEADS), f32),
        "ln_pre_mix": gain(ks[3]),
        "ln_post_mix": gain(ks[4]),
        "ln_pre_ffn": gain(ks[5]),
        "ln_post_ffn": gain(ks[6]),
        "w_in": jax.random.normal(ks[7], (DEPTH, D_MODEL, D_PROJ), f32) * D_MODEL ** -0.5,
        "b_forget": jax.random.uniform(ks[8], (DEPTH, FOX_HEADS), f32, minval=1.0, maxval=5.0),
        "sinks": 0.5 * jax.random.normal(ks[9], (DEPTH, SWA_Q_HEADS), f32),
        "w_out": jax.random.normal(ks[10], (DEPTH, D_MIX, D_MODEL), f32) * D_MIX ** -0.5,
        "w_gate_up": jax.random.normal(ks[11], (DEPTH, D_MODEL, 2 * D_FF), f32) * D_MODEL ** -0.5,
        "w_down": jax.random.normal(ks[12], (DEPTH, D_FF, D_MODEL), f32) * D_FF ** -0.5,
    }

def first_block(x, meta_tokens, rel_bias, ln_pre_mix, ln_post_mix, ln_pre_ffn, ln_post_ffn,
              w_in, b_forget, sinks, w_out, w_gate_up, w_down):
    B = x.shape[0]
    meta = jnp.broadcast_to(meta_tokens[None].astype(x.dtype), (B, N_META, D_MODEL))
    h = jnp.concatenate([meta, x], axis=1)
    L = h.shape[1]
    for layer in range(DEPTH):
        hn = rms_norm(h, ln_pre_mix[layer])
        proj = jnp.einsum('bld,dc->blc', hn, w_in[layer])
        q_a = proj[..., :OFF_QA].reshape(B, L, SWA_Q_HEADS, HEAD_DIM)
        k_a = proj[..., OFF_QA:OFF_KA].reshape(B, L, SWA_KV_HEADS, HEAD_DIM)
        v_a = proj[..., OFF_KA:OFF_VA].reshape(B, L, SWA_KV_HEADS, HEAD_DIM)
        q_b = proj[..., OFF_VA:OFF_QB].reshape(B, L, FOX_HEADS, HEAD_DIM)
        k_b = proj[..., OFF_QB:OFF_KB].reshape(B, L, FOX_HEADS, HEAD_DIM)
        v_b = proj[..., OFF_KB:OFF_VB].reshape(B, L, FOX_HEADS, HEAD_DIM)
        f_b = proj[..., OFF_VB:] + b_forget[layer].astype(proj.dtype)
        o_a = swa_sink_attention(q_a, k_a, v_a, sinks[layer], rel_bias)
        o_b = forgetting_attention(q_b, k_b, v_b, f_b)
        mix = jnp.concatenate([o_a.reshape(B, L, SWA_Q_W), o_b.reshape(B, L, FOX_W)], axis=-1)
        h = h + rms_norm(jnp.einsum('blc,cd->bld', mix, w_out[layer]), ln_post_mix[layer])
        hn = rms_norm(h, ln_pre_ffn[layer])
        gu = jnp.einsum('bld,df->blf', hn, w_gate_up[layer])
        ff = jnp.einsum('blf,fd->bld', jax.nn.silu(gu[..., :D_FF]) * gu[..., D_FF:], w_down[layer])
        h = h + rms_norm(ff, ln_post_ffn[layer])
    return h[:, N_META:]


DEPTH_2 = 2

CONF_WIDTH = 512
CONF_KERNEL = 31
SC_WIDTH = 512
SC_KERNEL = 3
MLA_HEADS = 8
QK_NOPE = 64
QK_ROPE = 32
V_HEAD = 64
Q_LORA = 384
KV_LORA = 256
MLA_WIDTH = MLA_HEADS * V_HEAD
ROPE_THETA = 10000.0
Q_BLOCK = 128
N_BRANCH = 3
LN_EPS = 1e-5
RMS_EPS = 1e-6
DEEPNORM_ALPHA = (2 * DEPTH_2) ** 0.25
DEEPNORM_BETA = (8 * DEPTH_2) ** -0.25
ADA_SCALE = 0.5

IN_SIZES = (2 * CONF_WIDTH, CONF_WIDTH, 3 * SC_WIDTH, SC_WIDTH, Q_LORA, KV_LORA, QK_ROPE, MLA_WIDTH, N_BRANCH * D_MODEL)
D_IN = 2 * CONF_WIDTH + CONF_WIDTH + 3 * SC_WIDTH + SC_WIDTH + Q_LORA + KV_LORA + QK_ROPE + MLA_WIDTH + N_BRANCH * D_MODEL


def layer_norm(x, g, b):
    x32 = x.astype(jnp.float32)
    mu = jnp.mean(x32, axis=-1, keepdims=True)
    var = jnp.mean(jnp.square(x32 - mu), axis=-1, keepdims=True)
    y = (x32 - mu) * lax.rsqrt(var + LN_EPS)
    return (y * g.astype(jnp.float32) + b.astype(jnp.float32)).astype(x.dtype)

def rms_norm_2(x, g):
    x32 = x.astype(jnp.float32)
    y = x32 * lax.rsqrt(jnp.mean(jnp.square(x32), axis=-1, keepdims=True) + RMS_EPS)
    return (y * g.astype(jnp.float32)).astype(x.dtype)

def causal_depthwise_conv(x, w):
    k_width, ch = w.shape
    return lax.conv_general_dilated(
        x, w.astype(x.dtype)[:, None, :], window_strides=(1,), padding=((k_width - 1, 0),),
        dimension_numbers=("NWC", "WIO", "NWC"), feature_group_count=ch)

def rope_tables(positions):
    inv_freq = ROPE_THETA ** (-jnp.arange(0, QK_ROPE, 2, dtype=jnp.float32) / QK_ROPE)
    ang = positions.astype(jnp.float32)[..., None] * inv_freq
    return jnp.cos(ang), jnp.sin(ang)

def apply_rope(x, cos, sin):
    cos = cos.astype(x.dtype)
    sin = sin.astype(x.dtype)
    x1, x2 = jnp.split(x, 2, axis=-1)
    return jnp.concatenate([x1 * cos - x2 * sin, x2 * cos + x1 * sin], axis=-1)

def causal_block_attention(q, k, v):
    b, s, h, dv = v.shape
    scale = (QK_NOPE + QK_ROPE) ** -0.5
    key_idx = jnp.arange(s)

    def one_block(i):
        start = i * Q_BLOCK
        qb = lax.dynamic_slice_in_dim(q, start, Q_BLOCK, axis=1)
        sc = jnp.einsum("bqhd,bkhd->bhqk", qb, k, preferred_element_type=jnp.float32) * scale
        q_idx = start + jnp.arange(Q_BLOCK)
        mask = key_idx[None, :] <= q_idx[:, None]
        sc = jnp.where(mask[None, None], sc, -jnp.inf)
        p = jax.nn.softmax(sc, axis=-1).astype(v.dtype)
        return jnp.einsum("bhqk,bkhd->bqhd", p, v)

    out = lax.map(one_block, jnp.arange(s // Q_BLOCK))
    return out.transpose(1, 0, 2, 3, 4).reshape(b, s, h, dv)

def hybrid_layer(x, c_act, cos, sin, w_ada, b_ada, w_in, conv_a_w, conv_a_b, ln_a_g, ln_a_b, w_a_out,
                 conv_b_w, w_b_out, q_norm_g, kv_norm_g, w_uq, w_ukv, w_c_out, w_o, ln_g, ln_b):
    b, s, _ = x.shape
    ada = c_act @ w_ada + b_ada
    shift, scale, gate = jnp.split(ada, 3, axis=-1)
    u = x * (1.0 + scale[:, None, :]) + shift[:, None, :]

    proj = jnp.einsum("bsd,dp->bsp", u, w_in)
    split_pts = [int(v) for v in np.cumsum(IN_SIZES)[:-1]]
    a_in, a_gate, b_in, b_gate, q_lat, kv_lat, k_rope, c_gate, merge_logits = jnp.split(proj, split_pts, axis=-1)

    a1, a2 = jnp.split(a_in, 2, axis=-1)
    a = a1 * jax.nn.sigmoid(a2)
    a = causal_depthwise_conv(a, conv_a_w) + conv_a_b
    a = jax.nn.silu(layer_norm(a, ln_a_g, ln_a_b))
    y_a = jnp.einsum("bsc,cd->bsd", a * jax.nn.silu(a_gate), w_a_out)

    xb, gb, gc = jnp.split(b_in, 3, axis=-1)
    yb = gb * causal_depthwise_conv(gc * xb, conv_b_w)
    y_b = jnp.einsum("bsc,cd->bsd", yb * jax.nn.silu(b_gate), w_b_out)

    q = jnp.einsum("bsr,rk->bsk", rms_norm_2(q_lat, q_norm_g), w_uq).reshape(b, s, MLA_HEADS, QK_NOPE + QK_ROPE)
    q_nope, q_pe = jnp.split(q, [QK_NOPE], axis=-1)
    q_pe = apply_rope(q_pe, cos[:, :, None, :], sin[:, :, None, :])
    kv = jnp.einsum("bsr,rk->bsk", rms_norm_2(kv_lat, kv_norm_g), w_ukv).reshape(b, s, MLA_HEADS, QK_NOPE + V_HEAD)
    k_nope, v = jnp.split(kv, [QK_NOPE], axis=-1)
    k_pe = apply_rope(k_rope, cos, sin)[:, :, None, :]
    qf = jnp.concatenate([q_nope, q_pe], axis=-1)
    kf = jnp.concatenate([k_nope, jnp.broadcast_to(k_pe, (b, s, MLA_HEADS, QK_ROPE))], axis=-1)
    o = causal_block_attention(qf, kf, v).reshape(b, s, MLA_WIDTH)
    y_c = jnp.einsum("bsc,cd->bsd", o * jax.nn.silu(c_gate), w_c_out)

    g_a, g_b, g_c = jnp.split(jax.nn.sigmoid(merge_logits), N_BRANCH, axis=-1)
    m = g_a * y_a + g_b * y_b + g_c * y_c
    out = jnp.einsum("bsd,de->bse", m, w_o)

    return layer_norm(DEEPNORM_ALPHA * x + gate[:, None, :] * out, ln_g, ln_b)

def second_inputs(seed: int = 0) -> dict:
    key = jax.random.key(seed)
    ks = jax.random.split(key, 24)
    L, D = DEPTH_2, D_MODEL

    def nrm(k, shape, scale):
        return jax.random.normal(k, shape, dtype=jnp.float32) * scale

    x = nrm(ks[0], (BATCH, SEQ, D), 1.0)
    c = nrm(ks[1], (BATCH, D), 1.0)
    offsets = jax.random.randint(ks[2], (BATCH, 1), 0, 1024, dtype=jnp.int32)
    positions = (jnp.arange(SEQ, dtype=jnp.int32)[None, :] + offsets).astype(jnp.int32)
    return {
        "x": x,
        "c": c,
        "positions": positions,
        "w_ada": nrm(ks[3], (L, D, 3 * D), ADA_SCALE * D ** -0.5),
        "b_ada": nrm(ks[4], (L, 3 * D), 0.02),
        "w_in": nrm(ks[5], (L, D, D_IN), D ** -0.5),
        "conv_a_w": nrm(ks[6], (L, CONF_KERNEL, CONF_WIDTH), CONF_KERNEL ** -0.5),
        "conv_a_b": nrm(ks[7], (L, CONF_WIDTH), 0.02),
        "ln_a_g": 1.0 + nrm(ks[8], (L, CONF_WIDTH), 0.02),
        "ln_a_b": nrm(ks[9], (L, CONF_WIDTH), 0.02),
        "w_a_out": nrm(ks[10], (L, CONF_WIDTH, D), DEEPNORM_BETA * CONF_WIDTH ** -0.5),
        "conv_b_w": nrm(ks[11], (L, SC_KERNEL, SC_WIDTH), SC_KERNEL ** -0.5),
        "w_b_out": nrm(ks[12], (L, SC_WIDTH, D), DEEPNORM_BETA * SC_WIDTH ** -0.5),
        "q_norm_g": 1.0 + nrm(ks[13], (L, Q_LORA), 0.02),
        "kv_norm_g": 1.0 + nrm(ks[14], (L, KV_LORA), 0.02),
        "w_uq": nrm(ks[15], (L, Q_LORA, MLA_HEADS * (QK_NOPE + QK_ROPE)), Q_LORA ** -0.5),
        "w_ukv": nrm(ks[16], (L, KV_LORA, MLA_HEADS * (QK_NOPE + V_HEAD)), KV_LORA ** -0.5),
        "w_c_out": nrm(ks[17], (L, MLA_WIDTH, D), DEEPNORM_BETA * MLA_WIDTH ** -0.5),
        "w_o": nrm(ks[18], (L, D, D), DEEPNORM_BETA * D ** -0.5),
        "ln_g": 1.0 + nrm(ks[19], (L, D), 0.02),
        "ln_b": nrm(ks[20], (L, D), 0.02),
    }

def second_block(x, c, positions, w_ada, b_ada, w_in, conv_a_w, conv_a_b, ln_a_g, ln_a_b, w_a_out,
              conv_b_w, w_b_out, q_norm_g, kv_norm_g, w_uq, w_ukv, w_c_out, w_o, ln_g, ln_b):
    c_act = jax.nn.silu(c)
    cos, sin = rope_tables(positions)
    h = x
    for l in range(DEPTH_2):
        h = hybrid_layer(h, c_act, cos, sin, w_ada[l], b_ada[l], w_in[l], conv_a_w[l], conv_a_b[l],
                         ln_a_g[l], ln_a_b[l], w_a_out[l], conv_b_w[l], w_b_out[l], q_norm_g[l],
                         kv_norm_g[l], w_uq[l], w_ukv[l], w_c_out[l], w_o[l], ln_g[l], ln_b[l])
    return h


def setup_inputs(seed=0):
    out = dict(first_inputs(seed))
    for name, value in second_inputs(seed + 1).items():
        if name != "x":
            out[name + "_2"] = value
    return out


def reference(
    x, meta_tokens, rel_bias, ln_pre_mix, ln_post_mix, ln_pre_ffn, ln_post_ffn, w_in, b_forget,
    sinks, w_out, w_gate_up, w_down, c_2, positions_2, w_ada_2, b_ada_2, w_in_2, conv_a_w_2,
    conv_a_b_2, ln_a_g_2, ln_a_b_2, w_a_out_2, conv_b_w_2, w_b_out_2, q_norm_g_2, kv_norm_g_2,
    w_uq_2, w_ukv_2, w_c_out_2, w_o_2, ln_g_2, ln_b_2,
):
    x = first_block(
        x, meta_tokens, rel_bias, ln_pre_mix, ln_post_mix, ln_pre_ffn, ln_post_ffn, w_in,
        b_forget, sinks, w_out, w_gate_up, w_down,
    )
    return second_block(
        x, c_2, positions_2, w_ada_2, b_ada_2, w_in_2, conv_a_w_2, conv_a_b_2, ln_a_g_2,
        ln_a_b_2, w_a_out_2, conv_b_w_2, w_b_out_2, q_norm_g_2, kv_norm_g_2, w_uq_2, w_ukv_2,
        w_c_out_2, w_o_2, ln_g_2, ln_b_2,
    )


_drawn_inputs = setup_inputs


def setup_inputs(seed=0):
    import zlib

    import numpy as np

    out = dict(_drawn_inputs(seed))
    spreads = {}
    factors = {'sinks': 8.0,
     'b_ada_2': 4.742,
     'conv_a_w_2': 3.335,
     'conv_a_b_2': 8.0,
     'ln_a_g_2': 8.0,
     'ln_a_b_2': 8.0,
     'w_a_out_2': 3.112,
     'q_norm_g_2': 8.0,
     'kv_norm_g_2': 8.0,
     'w_uq_2': 8.0,
     'w_ukv_2': 5.327,
     'w_c_out_2': 5.282}
    for name, (base, spread) in spreads.items():
        noise = np.random.default_rng([zlib.crc32(name.encode()), seed]).standard_normal(out[name].shape)
        drawn = base * np.exp(spread * noise) if base else spread * noise
        out[name] = __import__('jax').numpy.asarray(drawn.astype(out[name].dtype))
    for name, factor in factors.items():
        out[name] = (out[name] * factor).astype(out[name].dtype)
    return out
```

```python
import math
from contextlib import ExitStack

import numpy as np

import concourse.bass as bass
from concourse import mybir

ALU = mybir.AluOpType
ACT = mybir.ActivationFunctionType
AX = mybir.AxisListType
F32 = mybir.dt.float32
F32R = mybir.dt.float32r
I32 = mybir.dt.int32

P = 128
T = 512
NM = 16
D = 1024
KD = D // P
DH = 64
HEADS = 8
FF = 2816
KF = FF // P
NB = T // P
LAYERS = 2
CA, TAPS, CB = 512, 31, 3
KC = CA // P
BIG = 1e30
DEEPNORM_ALPHA = (2 * LAYERS) ** 0.25
MLA_SCALE = (64 + 32) ** -0.5
TWO_PI_1 = 6.28125
TWO_PI_2 = float(np.float32(int((2 * math.pi - TWO_PI_1) * 2 ** 20) / 2 ** 20))
TWO_PI_3 = 2 * math.pi - TWO_PI_1 - TWO_PI_2
ROUND = 1.5 * 2 ** 23

SLOT = 2048
S_IN, S_OUT, S_GU, S_DOWN = 0, 9, 13, 35
SLOTS1 = 46
L_BANK1 = 3 + 2 + 4 + 4 + 6
L_LAT, L_CG, L_UQ, L_UKV, L_A, L_B, L_M, L_WO = 0, 3, 5, 7, 8, 14, 22, 40
SLOTS2 = 44
N_SLOTS = SLOTS1 + LAYERS * SLOTS2

ROW_W, ROW_M = 384, 272
ROW = ROW_W + ROW_M

V_BADA, V_CAW = 0, 24
V_CAB = V_CAW + KC * TAPS
V_LAG, V_LAB = V_CAB + KC, V_CAB + 2 * KC
V_CBW = V_LAB + KC
V_QG = V_CBW + KC * CB
V_KG = V_QG + 3
V_LG, V_LB = V_KG + 2, V_KG + 2 + KD
NV2 = V_LB + KD


def tri(b):
    return b * (b + 1) // 2


class Tally:

    def __init__(self, base=0):
        self.base, self.n = base, 0

    def add(self, k=1):
        self.n += k

    def val(self, extra=0):
        return self.base + (self.n + extra)


class Fills:

    def __init__(self, base0=0, base1=0):
        self.f = [Tally(base0), Tally(base1)]

    def take(self, b):
        self.f[b].add()
        return self.f[b].val()


class Chain:

    def __init__(self, eng, sem, base=0):
        self.eng, self.sem, self.base, self.n = eng, sem, base, 0

    def mark(self, ins):
        ins.then_inc(self.sem, 1)
        self.n += 1
        return self.n

    def need(self, mark):
        self.eng.wait_ge(self.sem, self.base + mark)

    def link(self, ins):
        self.need(self.mark(ins))


TF1, TF2 = 4 + 1 + 1 + 3 + 3 + 4 + 4 + 22, 66
FILL1 = (3 + 2 + 4 + 4 + 4 + 22 + 1, 2 + 2 + 4 + 4 + 4 + 22 + 1)
FILL2 = 55
SQ1, SQ2 = 4 * KD, 5 + 2 * KC + 2 * KD
SQUARES2 = 5 + KC + KD
NORM1, NORM2 = 4, 6
SP1, SP2 = 2 * KD, KD + 5 + 3 * KC + KD
OWN1, OWN2 = 132, 177
UNITS = 2 * HEADS * NB


def program(nc, a, out, block1_only=False):
    ctx = ExitStack()
    with ctx:
        base = (nc.sbuf_base + 31) // 32 * 32
        at = [base]

        def sb_at(name, shape, dt, offset):
            assert offset + 4 * int(np.prod(shape[1:])) <= nc.sbuf_usable_end // 32 * 32, name
            return nc.alloc_sbuf_tensor_at(name, shape, dt, offset=offset)

        def sb(name, shape, dt=F32, offset=None):
            if offset is not None:
                at[0] = offset
            t = sb_at(name, shape, dt, at[0])
            at[0] += (4 * int(np.prod(shape[1:])) + 31) // 32 * 32
            return t

        def sem(name):
            return ctx.enter_context(nc.semaphore(name))

        h = sb("h", [P, KD, T])
        Xh = sb("Xh", [P, KD, T], F32R)
        Xl = sb("Xl", [P, KD, T], F32R)
        w_raw = sb("w_raw", [P, 2, SLOT])
        w_hi = sb("w_hi", [P, 2, SLOT], F32R)
        w_lo = sb("w_lo", [P, 2, SLOT], F32R)
        ident = sb("ident", [P, P])
        ones = sb("ones", [P, P])
        mask = sb("mask", [P, NM + 384 + P])
        vec1 = sb("vec1", [P, 4 * KD])
        vec2 = sb("vec2", [P, LAYERS, NV2])
        ropec = sb("ropec", [P, 4])
        ada = sb("ada", [P, LAYERS * 24])
        eps = sb("eps", [P, 2])
        rope_q = sb("rope_q", [P, T])
        sq = sb("sq", [P, 2, T])
        acc = sb("acc", [P, T])
        R = sb("R", [P, T])
        tmp = sb("tmp", [P, 2, T])
        nmax = sb("nmax", [P, 4])
        rsum = sb("rsum", [P, 4])
        rinv = sb("rinv", [P, 4])
        esink = sb("esink", [P, 4])
        ada_sum = sb("ada_sum", [P, 2])
        R0 = at[0]

        Qb = sb("Qb", [P, HEADS, T])
        Kb = sb("Kb", [P, HEADS, NM + T])
        Qa = sb("Qa", [P, 4, T])
        Ka = sb("Ka", [P, NM + T])
        V = sb("V", [P, NB, 640])
        Vm = sb("Vm", [NM, 640])
        bias0 = sb("bias0", [P, HEADS, NM + P])
        bias1 = sb("bias1", [P, HEADS, NM + 2 * P])
        o_p = at[0]
        Pr = sb("Pr", [P, 3, NM + T])
        PT = sb("PT", [P, NB, T])
        PTm = sb("PTm", [NM, T])
        o_end = at[0]
        brow = sb("brow", [P, 2, ROW], offset=o_p)
        tabb = sb("tabb", [33, HEADS, P])
        onehot = sb("onehot", [33, ROW])
        assert at[0] <= o_end
        cum_tri = sb("cum_tri", [P, NM + T], offset=o_end)
        metaT = sb("metaT", [P, KD, NM])
        meta_n = sb("meta_n", [P, KD, NM])
        Mh = sb("Mh", [P, KD, NM], F32R)
        Ml = sb("Ml", [P, KD, NM], F32R)
        sqm = sb("sqm", [P, KD, NM])
        accm = sb("accm", [P, NM])
        Rm = sb("Rm", [P, NM])
        wf = sb("wf", [P, KD, 8])
        wf_hi = sb("wf_hi", [P, KD, 8], F32R)
        wf_lo = sb("wf_lo", [P, KD, 8], F32R)
        bfb = sb("bfb", [P, 8])
        sinkb = sb("sinkb", [P, 8])
        nsink = sb("nsink", [P, 8])
        tab = sb("tab", [33, 8])
        fx = sb("fx", [P, NB + 1, 8])
        fa = sb("fa", [P, NB + 1, 8])
        ls = sb("ls", [P, NB + 1, 8])
        cum = sb("cum", [8, NM + T], offset=o_p + 8192 + 1024)
        ncum = sb("ncum", [8, NM + T], offset=o_p + 8192 + 1024 + 2112)

        act = sb("act", [P, KF, T], offset=R0)
        y = sb("y", [P, KD, T])
        act_h = sb("act_h", [P, 4, T], F32R)
        act_l = sb("act_l", [P, 4, T], F32R)
        ada_w = sb("ada_w", [P, 2, D])
        cact = sb("cact", [P, D])
        sgate = sb("sgate", [P, 2, T])
        pos = sb("pos", [P, T], I32, offset=R0 + KF * 4 * T)
        posf = sb("posf", [P, T])
        ada_prod = sb("ada_prod", [P, D])

        Q = sb("Q", [P, HEADS, T], offset=R0)
        K = sb("K", [P, HEADS, T])
        Vc = sb("Vc", [P, NB, T])
        o_pc = at[0]
        Pc = sb("Pc", [P, tri(NB) * P])
        PTc = sb("PTc", [P, tri(NB) * P])
        o_yc = at[0]
        yc_h = sb("yc_h", [P, KC, T], F32R)
        yc_l = sb("yc_l", [P, KC, T], F32R)
        o_cg = at[0]
        cg = sb("cg", [P, KC, T])
        o_ain = at[0]
        ain = sb("ain", [P, KC, TAPS - 1 + T])
        ag = sb("ag", [P, KC, T])
        sig = sb("sig", [P, T])
        lat = sb("lat", [P, 5, T], offset=o_ain)
        lat_h = sb("lat_h", [P, 5, T], F32R, offset=o_pc)
        lat_l = sb("lat_l", [P, 5, T], F32R)
        krope = sb("krope", [P, 2, T])
        assert at[0] <= o_cg
        bx = sb("bx", [P, KC, CB - 1 + T], offset=R0)
        o_cacc = at[0]
        cacc = sb("cacc", [P, KC, T])
        o_yb = at[0]
        yb_h = sb("yb_h", [P, KC, T], F32R)
        yb_l = sb("yb_l", [P, KC, T], F32R)
        o_m = at[0]
        btmp = sb("btmp", [P, 4, T])
        assert at[0] <= o_yc
        m = sb("m", [P, KD, T], offset=o_m)
        assert at[0] <= o_yc
        gt = sb("gt", [P, 4, T], offset=R0)
        assert at[0] <= o_cacc
        gt2 = sb("gt2", [P, 4, T], offset=o_yb)
        ya_h = sb("ya_h", [P, KC, T], F32R, offset=o_cg)
        ya_l = sb("ya_l", [P, KC, T], F32R)

        ps = ctx.enter_context(nc.psum_tensor("ps", [P, 8 * T], F32))

        def bank(b, n=T, p0=0, p1=P, c0=0):
            return ps[p0:p1, b * T + c0:b * T + c0 + n]

        def vec(L, c):
            return vec2[:, bass.ds(L, 1), c]

        B_O, B_ST = 6, 7

        consts_in = sem("consts_in")
        x_in = [sem(f"x_in{i}") for i in range(4)]
        w_landed = [sem("w_landed0"), sem("w_landed1")]
        w_hi_done = sem("w_hi_done")
        w_lo_done = sem("w_lo_done")
        tile_full = sem("tile_full")
        slot_done = sem("slot_done")
        bank_read = [sem("bank_read0"), sem("bank_read1")]
        sq_ready = sem("sq_ready")
        sq_added = sem("sq_added")
        sum_full = sem("sum_full")
        rt_done = sem("rt_done")
        t_ready = sem("t_ready")
        hi_done = sem("hi_done")
        lo_done = sem("lo_done")
        dve_own = sem("dve_own")
        act_own = sem("act_own")
        init_done = sem("init_done")
        meta_sq = sem("meta_sq")
        meta_sum = sem("meta_sum")
        meta_full = sem("meta_full")
        meta_rt = sem("meta_rt")
        meta_norm = sem("meta_norm")
        meta_hi = sem("meta_hi")
        meta_lo = sem("meta_lo")
        wf_ready = sem("wf_ready")
        wf_split = sem("wf_split")
        f_full = sem("f_full")
        f_biased = sem("f_biased")
        f_log = sem("f_log")
        ls_done = sem("ls_done")
        cum_full = sem("cum_full")
        cum_done = sem("cum_done")
        aug_in = sem("aug_in")
        nsink_done = sem("nsink_done")
        tabb_done = sem("tabb_done")
        brow_full = sem("brow_full")
        brow_done = sem("brow_done")
        brow_out = [sem("brow_out0"), sem("brow_out1")]
        bias_in = sem("bias_in")
        s_full = sem("s_full")
        max_done = sem("max_done")
        exp_done = sem("exp_done")
        p_done = sem("p_done")
        t_full = sem("t_full")
        pt_done = sem("pt_done")
        pv_done = sem("pv_done")
        o_hi = sem("o_hi")
        o_lo = sem("o_lo")
        ah_done = sem("ah_done")
        al_done = sem("al_done")
        down_read = sem("down_read")
        h_done = sem("h_done")
        adaw_in = [sem("adaw_in0"), sem("adaw_in1")]
        c_in = sem("c_in")
        cact_done = sem("cact_done")
        ada_done = sem("ada_done")
        ada_copied = sem("ada_copied")
        pos_in = sem("pos_in")
        ang_done = sem("ang_done")
        rope_done = sem("rope_done")
        out_done = sem("out_done")
        kpe_done = sem("kpe_done")
        kpe_both = sem("kpe_both")
        kpe_spread = sem("kpe_spread")
        s2_full = sem("s2_full")
        max2_done = sem("max2_done")
        scores_seen = sem("scores_seen")
        pool_step = sem("pool_step")
        exp2_done = sem("exp2_done")
        p2_done = sem("p2_done")
        t2_full = sem("t2_full")
        pt2_done = sem("pt2_done")
        pv2_done = sem("pv2_done")
        conv_done = sem("conv_done")
        zc_ready = sem("zc_ready")
        ln_mid = sem("ln_mid")
        ya_act = sem("ya_act")
        ln_out = sem("ln_out")
        h_scaled = sem("h_scaled")

        scratch = nc.dram_tensor("bias_scratch", (HEADS, P * ROW + ROW), F32, kind="Internal").ap()
        block = ctx.enter_context(nc.Block())

        N_CONST = 13

        @block.sync
        def _(sp):
            for i in range(4):
                sp.dma_start(h[:, 2 * i:2 * i + 2, :], a["xT"][:, 2 * i:2 * i + 2, :]).then_inc(x_in[i], 16)

            def load(g, par):
                sp.dma_start(w_raw[:, par, :], a["w"][bass.ds(g, 1), :, :].rearrange("a p n -> p (a n)")
                             ).then_inc(w_landed[par], 16)

            for g in range(2):
                load(g, g)
            with sp.Fori(1, (SLOTS1 if block1_only else N_SLOTS) // 2) as i:
                for par in range(2):
                    sp.wait_ge(w_lo_done, 2 * i + (par - 1))
                    load(2 * i + par, par)
            if block1_only:
                sp.wait_ge(h_done, 2 * KD)
            else:
                sp.wait_ge(ln_out, LAYERS * KD)
            sp.dma_start(out, h[:, :, :]).then_inc(out_done, 16)
            sp.wait_ge(out_done, 16)

        @block.gpsimd
        def _(pool):
            for dst, src in ((ident, "ident"), (mask, "mask"), (vec1, "vec1"), (vec2, "vec2"), (ropec, "ropec"),
                             (cum_tri, "cum_tri"), (metaT, "metaT"), (wf, "wf"), (onehot, "onehot")):
                view = dst[:, :, :] if len(dst.shape) == 3 else dst[:, :]
                pool.dma_start(view, a[src]).then_inc(consts_in, 16)
            pool.dma_start(tab[0:32, :], a["rel_bias"]).then_inc(consts_in, 16)
            pool.dma_start(tab[32:33, :], a["outside"]).then_inc(consts_in, 16)
            pool.dma_start(bfb[:, :], a["b_forget"].partition_broadcast(P)).then_inc(consts_in, 16)
            pool.dma_start(sinkb[:, :], a["sinks"].partition_broadcast(P)).then_inc(consts_in, 16)

            def add_up(n, norm, first, src, ready, count):
                if first:
                    pool.wait_ge(consts_in, 16 * N_CONST)
                pool.wait_ge(ready, count)
                if first:
                    if not (isinstance(norm, int) and norm == 0):
                        pool.wait_ge(sum_full, norm)
                    pool.sem_inc(pool_step, 1)
                    nc.gpsimd.tensor_copy(acc[:, :], src).then_inc(sq_added, 1)
                else:
                    pool.wait_ge(sq_added, n)
                    nc.gpsimd.tensor_tensor(acc[:, :], acc[:, :], src, ALU.add).then_inc(sq_added, 1)

            def add_squares(norm):
                for j in range(KD):
                    n = KD * norm + j
                    add_up(n, norm, j == 0, sq[:, n % 2, :], sq_ready, n + 1)

            add_squares(0)
            for hd in range(HEADS):
                pool.wait_ge(brow_done, hd + 1)
                pool.dma_start(scratch[hd, 0:P * ROW].rearrange("(p r) -> p r", r=ROW), brow[:, hd % 2, :]
                               ).then_inc(brow_out[hd % 2], 16)
            for s in brow_out:
                pool.wait_ge(s, 16 * HEADS // 2)

            def skew(dst, c0, n):
                src = scratch[:, c0:c0 + P * (ROW - 1)].rearrange("h (p r) -> p h r", r=ROW - 1)[:, :, 0:n]
                pool.dma_start(dst, src).then_inc(bias_in, 16)

            skew(bias0[:, :, 0:NM], ROW_W + P - 1 + P, NM)
            skew(bias0[:, :, NM:NM + P], P - 1 + P, P)
            skew(bias1[:, :, 0:NM], ROW_W + P - 1, NM)
            skew(bias1[:, :, NM:NM + 2 * P], P - 1, 2 * P)
            pool.wait_ge(cum_done, 2)
            pool.dma_start(Kb[64:65, :, :], cum[:, :]).then_inc(aug_in, 16)
            pool.dma_start(Qb[65:66, :, :], ncum[:, NM:NM + T]).then_inc(aug_in, 16)
            add_squares(1)
            add_squares(2)
            if not block1_only:
                pool.wait_ge(slot_done, S_GU + 1)
                pool.dma_start(cact[:, :], a["c"].partition_broadcast(P)).then_inc(c_in, 16)
                pool.dma_start(pos[:, :], a["positions"].partition_broadcast(P)).then_inc(pos_in, 16)

                def load_ada(t, par):
                    pool.dma_start(ada_w[:, par, :], a["w_ada"][bass.ds(t, 1), :, :].rearrange("a p n -> p (a n)")
                                   ).then_inc(adaw_in[par], 16)

                for par in range(2):
                    load_ada(par, par)
                with pool.Fori(1, LAYERS * 12) as i:
                    for par in range(2):
                        pool.wait_ge(ada_done, 2 * i + par)
                        load_ada(2 * i + par, par)
            add_squares(3)
            if block1_only:
                return
            with pool.Fori(0, LAYERS) as L:
                n, norm = SQ1 + SQ2 * L, NORM1 + NORM2 * L
                nsq = SQ1 + SQUARES2 * L
                for j in range(5):
                    add_up(n + j, norm + int(j >= 3), j in (0, 3), sq[:, j % 2, :], sq_ready, nsq + (j + 1))
                pool.wait_ge(aug_in, 32)
                pool.wait_ge(kpe_both, L + 1)
                pool.wait_ge(sq_added, n + 5)
                pool.sem_inc(pool_step, 1)
                nc.gpsimd.tensor_copy(K[DH:P, :, :], krope[DH:P, 0:1, :].to_broadcast([DH, HEADS, T])
                                      ).then_inc(kpe_spread, 1)
                pool.wait_ge(kpe_spread, L + 1)
                for j in range(KC):
                    add_up(n + (5 + j), norm + 2, j == 0, cacc[:, j, :], conv_done, KC * L + (j + 1))
                for j in range(KC):
                    add_up(n + (5 + KC + j), norm + 3, j == 0, sq[:, j % 2, :], sq_ready, nsq + (5 + j + 1))
                for j in range(KD):
                    add_up(n + (5 + 2 * KC + j), norm + 4, j == 0, h[:, j, :], bank_read[j % 2],
                           FILL1[j % 2] + FILL2 * L + (FILL2 - 4 + j // 2 + 1))
                for j in range(KD):
                    add_up(n + (5 + 2 * KC + KD + j), norm + 5, j == 0, sq[:, j % 2, :], sq_ready,
                           nsq + (5 + KC + j + 1))

        @block.tensor
        def _(pe):
            def wait_fill(fills, b):
                v = fills.f[b].val()
                if not (isinstance(v, int) and v == 0):
                    pe.wait_ge(bank_read[b], v)
                fills.take(b)

            def mm3(o_, whi, wlo, xhi, xlo, start, stop):
                nc.tensor.matmul(o_, whi, xhi, start=start, stop=False)
                nc.tensor.matmul(o_, whi, xlo, start=False, stop=False)
                return nc.tensor.matmul(o_, wlo, xhi, start=False, stop=stop)

            def w(par, c0, n=P):
                return w_hi[:, par, c0:c0 + n], w_lo[:, par, c0:c0 + n]

            def pair_tile(par, j, fills, xwait=None):
                wait_fill(fills, j)
                for k in range(KD):
                    if xwait is not None:
                        pe.wait_ge(*xwait(k))
                    whi, wlo = w(par, k * 2 * P + j * P)
                    last = mm3(bank(j), whi, wlo, Xh[:, k, :], Xl[:, k, :], k == 0, k == KD - 1)
                return last

            def meta_tile(par, j, b):
                for k in range(KD):
                    whi, wlo = w(par, k * 2 * P + j * P)
                    last = mm3(bank(b, NM), whi, wlo, Mh[:, k, :], Ml[:, k, :], k == 0, k == KD - 1)
                return last

            def pair_slot(g, par, fills, xwait=None, meta=False):
                pe.wait_ge(w_lo_done, g + 1)
                for j in range(2):
                    last = pair_tile(par, j, fills, xwait if j == 0 else None)
                    if meta:
                        last = meta_tile(par, j, 2 + j)
                    last.then_inc(tile_full if j == 0 else slot_done, 1)

            def v_tiles(par, c0, n, fills, first_bank):
                for t in range(NB):
                    b = (first_bank + t) % 2
                    wait_fill(fills, b)
                    for k in range(KD):
                        whi, wlo = w(par, k * 2 * P + c0, n)
                        last = mm3(bank(b, n), Xh[:, k, t * P:(t + 1) * P], Xl[:, k, t * P:(t + 1) * P],
                                   whi, wlo, k == 0, k == KD - 1)
                    if t == NB - 1:
                        for k in range(KD):
                            whi, wlo = w(par, k * 2 * P + c0, n)
                            last = mm3(bank(3, n, 0, NM), Mh[:, k, :], Ml[:, k, :], whi, wlo, k == 0, k == KD - 1)
                    last.then_inc(slot_done if t == NB - 1 else tile_full, 1)

            def sums(norm, n_added):
                pe.wait_ge(sq_added, n_added)
                if not (isinstance(norm, int) and norm == 0):
                    pe.wait_ge(rt_done, norm)
                nc.tensor.matmul(bank(B_ST), ones[:, :], acc[:, :], start=True, stop=True).then_inc(sum_full, 1)

            pe.wait_ge(init_done, 1)
            sums(0, KD)
            pe.wait_ge(meta_sum, 1)
            nc.tensor.matmul(bank(B_O, NM), ones[:, :], accm[:, :], start=True, stop=True).then_inc(meta_full, 1)
            pe.wait_ge(tabb_done, 1)
            pe.wait_ge(consts_in, 16 * N_CONST)
            for hd in range(HEADS):
                b = 2 + 2 * (hd % 2)
                if hd >= 2:
                    pe.wait_ge(brow_done, hd - 1)
                nc.tensor.matmul(bank(b, ROW_W), tabb[:, hd, :], onehot[:, 0:ROW_W], start=True, stop=True)
                nc.tensor.matmul(bank(b + 1, ROW_M), tabb[:, hd, :], onehot[:, ROW_W:ROW], start=True, stop=True
                                 ).then_inc(brow_full, 1)

            fills = Fills()
            pe.wait_ge(brow_done, HEADS)
            pe.wait_ge(w_lo_done, 1)
            pair_tile(0, 0, fills, xwait=lambda k: (lo_done, k + 1))
            pe.wait_ge(meta_lo, 1)
            meta_tile(0, 0, 2).then_inc(tile_full, 1)
            v_tiles(0, P, P, fills, 1)
            pe.wait_ge(wf_split, 1)
            for t in range(NB):
                for k in range(KD):
                    mm3(bank(B_O, 8, c0=32 + 8 * t), Xh[:, k, t * P:(t + 1) * P], Xl[:, k, t * P:(t + 1) * P],
                        wf_hi[:, k, :], wf_lo[:, k, :], k == 0, k == KD - 1)
            for k in range(KD):
                last = mm3(bank(B_O, 8, 0, NM, c0=32 + 8 * NB), Mh[:, k, :], Ml[:, k, :],
                           wf_hi[:, k, :], wf_lo[:, k, :], k == 0, k == KD - 1)
            last.then_inc(f_full, 1)
            pair_slot(1, 1, fills, meta=True)
            pair_slot(2, 0, fills, meta=True)
            pe.wait_ge(ls_done, 1)
            nc.tensor.matmul(bank(B_O, NM, 0, 8), ls[0:NM, NB, :], cum_tri[0:NM, 0:NM], start=True, stop=True)
            nc.tensor.matmul(bank(B_ST, T, 0, 8), ls[0:NM, NB, :], cum_tri[0:NM, NM:NM + T], start=True, stop=False)
            for t in range(NB):
                last = nc.tensor.matmul(bank(B_ST, T - P * t, 0, 8, c0=P * t), ls[:, t, :], cum_tri[:, 0:T - P * t],
                                        start=False, stop=t == NB - 1)
            last.then_inc(cum_full, 1)
            for g in (3, 4):
                pe.wait_ge(w_lo_done, g + 1)
                v_tiles(g % 2, 0, 2 * P, fills, 0)
            for g in range(5, 9):
                pair_slot(g, g % 2, fills)

            def score_banks(u):
                return 2 * (u % 3)

            def fox_scores(u):
                hd, b = u // NB, u % NB
                c = score_banks(u)
                q = Qb[0:66, hd, b * P:(b + 1) * P]
                nc.tensor.matmul(bank(c, NM, c0=T - NM), q, Kb[0:66, hd, 0:NM], start=True, stop=True)
                return nc.tensor.matmul(bank(c + 1, P * (b + 1)), q, Kb[0:66, hd, NM:NM + P * (b + 1)],
                                        start=True, stop=True)

            def swa_head(u):
                i = (u - UNITS // 2) // NB
                return i // 2, i % 2

            def swa_scores(u):
                i, kv = swa_head(u)
                b = u % NB
                c = score_banks(u)
                r = slice(kv * DH, (kv + 1) * DH)
                q = Qa[r, i, b * P:(b + 1) * P]
                k0 = max(b - 1, 0)
                nc.tensor.matmul(bank(c, NM, c0=T - NM), q, Ka[r, 0:NM], start=True, stop=True)
                return nc.tensor.matmul(bank(c + 1, P * (b + 1 - k0)), q, Ka[r, NM + P * k0:NM + P * (b + 1)],
                                        start=True, stop=True)

            def scores(u):
                if u >= 3:
                    pe.wait_ge(pt_done, u - 2)
                (fox_scores if u < UNITS // 2 else swa_scores)(u).then_inc(s_full, 1)

            def transposes(u):
                b = u % NB
                c = score_banks(u)
                n = b + 1 if u < UNITS // 2 else min(b, 1) + 1
                pe.wait_ge(p_done, u + 1)
                nc.tensor.transpose(bank(c, P, 0, NM), Pr[:, u % 3, 0:NM], ident[:, :])
                for k in range(n):
                    last = nc.tensor.transpose(bank(c + 1, P, c0=P * k), Pr[:, u % 3, NM + P * k:NM + P * (k + 1)],
                                               ident[:, :])
                last.then_inc(t_full, 1)

            def fox_pv(hd):
                e = hd % 2
                cols = slice(P + DH * hd, P + DH * (hd + 1))
                nc.tensor.matmul(bank(B_O, T, DH * e, DH * (e + 1)), Vm[0:NM, cols], PTm[0:NM, :], start=True, stop=False)
                for k in range(NB):
                    last = nc.tensor.matmul(bank(B_O, T - P * k, DH * e, DH * (e + 1), c0=P * k), V[:, k, cols],
                                            PT[:, k, P * k:T], start=False, stop=k == NB - 1)
                return last

            def swa_pv(kv):
                cols = slice(DH * kv, DH * (kv + 1))
                nc.tensor.matmul(bank(B_O, T, DH * kv, DH * (kv + 1)), Vm[0:NM, cols], PTm[0:NM, :],
                                 start=True, stop=False)
                for b in range(NB):
                    o_ = bank(B_O, P, DH * kv, DH * (kv + 1), c0=P * b)
                    if b:
                        nc.tensor.matmul(o_, V[:, b - 1, cols], PT[:, 0, P * b:P * (b + 1)], start=False, stop=False)
                    last = nc.tensor.matmul(o_, V[:, b, cols], PT[:, min(b, 1), P * b:P * (b + 1)],
                                            start=False, stop=b == NB - 1)
                return last

            def values(hd):
                pe.wait_ge(pt_done, NB * (hd + 1))
                if hd >= 2 and hd % 2 == 0:
                    pe.wait_ge(o_lo, hd // 2)
                (fox_pv(hd) if hd < HEADS else swa_pv(hd % 2)).then_inc(pv_done, 1)

            for b in range(2):
                pe.wait_ge(bank_read[b], fills.f[b].val())
            pe.wait_ge(cum_done, 2)
            pe.wait_ge(aug_in, 32)
            for u in range(3):
                scores(u)
            for u in range(UNITS):
                transposes(u)
                if 1 <= u < UNITS - 2:
                    scores(u + 2)
                if u % NB == NB - 1:
                    values(u // NB)
            pe.wait_ge(pt_done, UNITS)
            for g in range(S_OUT, S_GU):
                pair_slot(g, g % 2, fills, xwait=(lambda k: (o_lo, HEADS)) if g == S_OUT else None)
            sums(1, 2 * KD)
            sums(2, 3 * KD)
            for k in range(KD):
                pe.wait_ge(lo_done, KD + k + 1)
            with pe.Fori(0, KF // 2) as i:
                lf = Fills(fills.f[0].val() + 2 * i, fills.f[1].val() + 2 * i)
                for s in range(2):
                    pair_slot(S_GU + s + 2 * i, (S_GU + s) % 2, lf)
            for b in range(2):
                fills.f[b].add(KF)
                wait_fill(fills, b)

            def down_slot(g, par, k0, start, stop):
                pe.wait_ge(w_lo_done, g + 1)
                for kk in range(2):
                    pe.wait_ge(al_done, k0 + kk + 1)
                    r = 2 * ((par + S_DOWN) % 2) + kk
                    for j in range(KD):
                        whi, wlo = w(par, kk * D + j * P)
                        last = mm3(bank(j), whi, wlo, act_h[:, r, :], act_l[:, r, :],
                                   start and kk == 0, stop and kk == 1)
                last.then_inc(slot_done, 1)

            pe.wait_ge(rt_done, 3)
            down_slot(S_DOWN, S_DOWN % 2, 0, True, False)
            with pe.Fori(0, 4) as i:
                for s in range(2):
                    down_slot(S_DOWN + 1 + s + 2 * i, (S_DOWN + 1 + s) % 2, 2 + 2 * s + 4 * i, False, False)
            for s in (9, 10):
                down_slot(S_DOWN + s, (S_DOWN + s) % 2, 2 * s, False, s == 10)
            pe.wait_ge(down_read, KD - 2)
            sums(3, 4 * KD)
            assert (fills.f[0].n, fills.f[1].n) == FILL1, (fills.f[0].n, fills.f[1].n)
            if block1_only:
                return

            with pe.Fori(0, LAYERS) as L:
                fills = Fills(FILL1[0] + FILL2 * L, FILL1[1] + FILL2 * L)
                G = SLOTS1 + SLOTS2 * L
                nsum = NORM1 + NORM2 * L
                nadd = SQ1 + SQ2 * L
                split0 = SP1 + SP2 * L
                for s in range(3):
                    pair_slot(G + s, s % 2, fills, xwait=(lambda k: (lo_done, split0 + (k + 1))) if s == 0 else None)
                    if s == 1:
                        sums(nsum, nadd + 3)
                pair_slot(G + L_CG, L_CG % 2, fills)
                sums(nsum + 1, nadd + 5)
                pair_slot(G + (L_CG + 1), (L_CG + 1) % 2, fills)
                for s in range(2):
                    g, par = G + (L_UQ + s), (L_UQ + s) % 2
                    pe.wait_ge(w_lo_done, g + 1)
                    if s == 0:
                        pe.wait_ge(lo_done, split0 + (KD + 3))
                    for j in range(4):
                        wait_fill(fills, j % 2)
                        for k in range(3):
                            whi, wlo = w(par, k * 4 * P + j * P)
                            last = mm3(bank(j % 2), whi, wlo, lat_h[:, k, :], lat_l[:, k, :], k == 0, k == 2)
                        last.then_inc(slot_done if j == 3 else tile_full, 1)
                g, par = G + L_UKV, L_UKV % 2
                pe.wait_ge(w_lo_done, g + 1)
                pe.wait_ge(lo_done, split0 + (KD + 5))
                for j in range(4):
                    wait_fill(fills, j % 2)
                    for k in range(2):
                        whi, wlo = w(par, k * 4 * P + j * P)
                        last = mm3(bank(j % 2), whi, wlo, lat_h[:, 3 + k, :], lat_l[:, 3 + k, :], k == 0, k == 1)
                    last.then_inc(tile_full, 1)
                for t in range(NB):
                    wait_fill(fills, t % 2)
                    for k in range(2):
                        whi, wlo = w(par, D + k * T, T)
                        last = mm3(bank(t % 2), lat_h[:, 3 + k, t * P:(t + 1) * P], lat_l[:, 3 + k, t * P:(t + 1) * P],
                                   whi, wlo, k == 0, k == 1)
                    last.then_inc(slot_done if t == NB - 1 else tile_full, 1)

                U0 = NB * HEADS * L
                for b in range(2):
                    pe.wait_ge(bank_read[b], fills.f[b].val())
                pe.wait_ge(kpe_spread, L + 1)

                def half_slot(i, j):
                    if i < 6:
                        if j == 0:
                            pe.wait_ge(w_lo_done, G + (L_A + i) + 1)
                        pair_tile((L_A + i) % 2, j, fills).then_inc(tile_full if j == 0 else slot_done, 1)

                for hd in range(HEADS):
                    for b in range(NB):
                        if hd:
                            pe.wait_ge(pt2_done, U0 + (NB * (hd - 1) + b + 1))
                        nc.tensor.matmul(bank(2 + b, P * (b + 1)), Q[:, hd, b * P:(b + 1) * P],
                                         K[:, hd, 0:P * (b + 1)], start=True, stop=True).then_inc(s2_full, 1)
                    half_slot(hd, 0)
                    for b in range(NB):
                        pe.wait_ge(p2_done, U0 + (NB * hd + b + 1))
                        for k in range(b + 1):
                            last = nc.tensor.transpose(bank(2 + b, P, c0=P * k),
                                                       Pc[:, P * (tri(b) + k):P * (tri(b) + k + 1)], ident[:, :])
                        last.then_inc(t2_full, 1)
                    half_slot(hd, 1)
                    pe.wait_ge(pt2_done, U0 + NB * (hd + 1))
                    if hd and hd % 2 == 0:
                        pe.wait_ge(t_ready, split0 + (KD + 5 + hd // 2))
                    for b in range(NB):
                        for k in range(b + 1):
                            last = nc.tensor.matmul(bank(B_O, P, DH * (hd % 2), DH * (hd % 2 + 1), c0=P * b),
                                                    Vc[:, k, DH * hd:DH * (hd + 1)],
                                                    PTc[:, P * (tri(b) + k):P * (tri(b) + k + 1)],
                                                    start=k == 0, stop=k == b)
                    last.then_inc(pv2_done, 1)

                for s in range(L_B, L_M):
                    pair_slot(G + s, s % 2, fills)

                def y_slot(s, yh, yl, ready):
                    pe.wait_ge(w_lo_done, G + (s + 1))
                    for j in range(4):
                        wait_fill(fills, j % 2)
                        for k in range(KC):
                            if j == 0:
                                pe.wait_ge(lo_done, split0 + (ready - KC + 1 + k))
                            whi, wlo = w(s % 2, k * 4 * P + j * P)
                            last = mm3(bank(j % 2), whi, wlo, yh[:, k, :], yl[:, k, :], k == 0, k == KC - 1)
                        last.then_inc(slot_done if j == 3 else tile_full, 1)

                for br, (yh, yl) in enumerate(((yc_h, yc_l), (yb_h, yb_l))):
                    for half in range(2):
                        s = L_M + 6 * br + 3 * half
                        pair_slot(G + s, s % 2, fills)
                        pair_slot(G + (s + 1), (s + 1) % 2, fills)
                        y_slot(s + 2, yh, yl, KD + 5 + KC * (br + 1))
                for s in range(4):
                    pair_slot(G + (L_M + 12 + s), (L_M + 12 + s) % 2, fills)
                    if s < 2:
                        sums(nsum + (2 + s), nadd + (5 + KC * (s + 1)))
                for s in range(2):
                    y_slot(L_M + 16 + s, ya_h, ya_l, KD + 5 + 3 * KC)
                for s in range(4):
                    pair_slot(G + (L_WO + s), (L_WO + s) % 2, fills,
                              xwait=(lambda k: (lo_done, split0 + (KD + 5 + 3 * KC + k + 1))) if s == 0 else None)
                sums(nsum + 4, nadd + (5 + 2 * KC + KD))
                sums(nsum + 5, nadd + (5 + 2 * KC + 2 * KD))
                assert fills.f[0].n == FILL2 and fills.f[1].n == FILL2, (fills.f[0].n, fills.f[1].n)

        @block.scalar
        def _(sc):
            def act_(o_, i_, f, **kw):
                return nc.scalar.activation(o_, i_, f, **kw)

            def slot_hi(g, half, par):
                sc.wait_ge(w_landed[par], 16 * half + 16)
                if not (isinstance(g, int) and g < 2):
                    sc.wait_ge(slot_done, g - 1)
                act_(w_hi[:, par, :], w_raw[:, par, :], ACT.Copy).then_inc(w_hi_done, 1)

            def first_block_hi(g):
                slot_hi(g, g // 2, g % 2)

            def square(src, n, k):
                if not (isinstance(n, int) and n < 2):
                    sc.wait_ge(sq_added, n - 1)
                act_(sq[:, k % 2, :], src, ACT.Square).then_inc(sq_ready, 1)

            def root(norm, width, e):
                sc.wait_ge(sum_full, norm + 1)
                act_(R[:, :], bank(B_ST), ACT.Sqrt, scale=1.0 / width, bias=eps[:, e:e + 1]).then_inc(rt_done, 1)

            def mean(norm, width):
                sc.wait_ge(sum_full, norm + 1)
                act_(R[:, :], bank(B_ST), ACT.Copy, scale=1.0 / width).then_inc(rt_done, 1)

            def hi(dst, n, k):
                sc.wait_ge(t_ready, n + 1)
                act_(dst, tmp[:, k % 2, :], ACT.Copy).then_inc(hi_done, 1)

            def full(tf, g, last):
                if last:
                    sc.wait_ge(slot_done, g + 1)
                else:
                    tf.add()
                    sc.wait_ge(tile_full, tf.val())

            tf = Tally()
            sc.wait_ge(init_done, 1)
            for j in range(KD):
                sc.wait_ge(x_in[j // 2], 16)
                square(h[:, j, :], j, j)
            sc.wait_ge(consts_in, 16 * N_CONST)
            act_(sqm[:, :, :], metaT[:, :, :], ACT.Square).then_inc(meta_sq, 1)
            root(0, D, 0)
            sc.wait_ge(meta_full, 1)
            act_(Rm[:, :], bank(B_O, NM), ACT.Sqrt, scale=1.0 / D, bias=eps[:, 0:1]).then_inc(meta_rt, 1)
            first_block_hi(0)
            act_(wf_hi[:, :, :], wf[:, :, :], ACT.Copy).then_inc(wf_ready, 1)
            for j in range(KD):
                hi(Xh[:, j, :], j, j)
            sc.wait_ge(meta_norm, KD)
            act_(Mh[:, :, :], meta_n[:, :, :], ACT.Copy).then_inc(meta_hi, 1)
            for hd in range(HEADS):
                sc.wait_ge(brow_full, hd + 1)
                if hd >= 2:
                    sc.wait_ge(brow_out[hd % 2], 16 * (hd // 2))
                b = 2 + 2 * (hd % 2)
                act_(brow[:, hd % 2, 0:ROW_W], bank(b, ROW_W), ACT.Copy)
                act_(brow[:, hd % 2, ROW_W:ROW], bank(b + 1, ROW_M), ACT.Copy).then_inc(brow_done, 1)
            first_block_hi(1)

            full(tf, 0, False)
            act_(Ka[:, NM:NM + T], bank(0), ACT.Copy)
            act_(Ka[:, 0:NM], bank(2, NM), ACT.Copy).then_inc(bank_read[0], 1)
            tf.add(3)
            for s in (1, 2):
                first_block_hi(s + 1)
                for j in range(2):
                    full(tf, s, j == 1)
                    for e in range(2):
                        hd = 4 * (s - 1) + 2 * j + e
                        act_(Kb[0:DH, hd, 0:NM], bank(2 + j, NM, DH * e, DH * (e + 1)), ACT.Copy)
                        last = act_(Kb[0:DH, hd, NM:NM + T], bank(j, T, DH * e, DH * (e + 1)), ACT.Copy)
                    last.then_inc(bank_read[j], 1)
                if s == 1:
                    sc.wait_ge(f_biased, 2)
                    act_(fa[:, :, :], fx[:, :, :], ACT.Abs).then_inc(act_own, 1)
                    sc.wait_ge(act_own, 1)
                    act_(fa[:, :, :], fa[:, :, :], ACT.Exp, scale=-1.0).then_inc(act_own, 1)
                    sc.wait_ge(act_own, 2)
                    act_(fa[:, :, :], fa[:, :, :], ACT.Ln, bias=ones[:, 0:1]).then_inc(f_log, 1)
            for s in (3, 4):
                first_block_hi(s + 1)
                tf.add(3)
            for s in range(5, 9):
                first_block_hi(s + 1)
                for j in range(2):
                    full(tf, s, j == 1)
                    if s < 7:
                        for e in range(2):
                            hd = 4 * (s - 5) + 2 * j + e
                            last = act_(Qb[0:DH, hd, :], bank(j, T, DH * e, DH * (e + 1)), ACT.Copy, scale=-0.125)
                    else:
                        last = act_(Qa[:, 2 * (s - 7) + j, :], bank(j), ACT.Copy, scale=-0.125)
                    last.then_inc(bank_read[j], 1)

            def exp_unit(u):
                b, k = u % NB, u % 4
                swa = u >= UNITS // 2
                n = NM + P * ((min(b, 1) if swa else b) + 1)
                c0 = 2 * (u % 3) * T + T - NM
                sc.wait_ge(max_done, u + 1)
                if u >= 3:
                    sc.wait_ge(t_full, u - 2)
                act_(Pr[:, u % 3, 0:n], ps[:, c0:c0 + n], ACT.Exp, scale=-1.0, bias=nmax[:, k:k + 1],
                     accum_out=rsum[:, k:k + 1]).then_inc(exp_done, 1)
                if swa:
                    i = (u - UNITS // 2) // NB
                    hs = i // 2 + 4 * (i % 2)
                    act_(esink[:, k:k + 1], nmax[:, k:k + 1], ACT.Exp, bias=sinkb[:, hs:hs + 1]).then_inc(exp_done, 1)

            def pt_unit(u):
                b = u % NB
                c = 2 * (u % 3)
                n = b + 1 if u < UNITS // 2 else min(b, 1) + 1
                sc.wait_ge(t_full, u + 1)
                if u >= NB and b == 0:
                    sc.wait_ge(pv_done, u // NB)
                act_(PT[:, 0:n, b * P:(b + 1) * P],
                     bank(c + 1, P * n).rearrange("p (k q) -> p k q", k=n), ACT.Copy)
                act_(PTm[0:NM, b * P:(b + 1) * P], bank(c, P, 0, NM), ACT.Copy).then_inc(pt_done, 1)

            def out_hi(i):
                sc.wait_ge(pv_done, 2 * (i + 1))
                act_(Xh[:, (4 + i) % 8, :], bank(B_O), ACT.Copy).then_inc(o_hi, 1)

            exp_unit(0)
            exp_unit(1)
            for u in range(UNITS):
                pt_unit(u)
                if u + 2 < UNITS:
                    exp_unit(u + 2)
                if u % (2 * NB) == 0 and u:
                    out_hi(u // (2 * NB) - 1)
            out_hi(7)

            for s in range(S_OUT, S_GU):
                first_block_hi(s + 1)
                for j in range(2):
                    full(tf, s, j == 1)
                    n = KD + 2 * (s - S_OUT) + j
                    square(bank(j), n, n)
                    act_(y[:, n - KD, :], bank(j), ACT.Copy).then_inc(bank_read[j], 1)
            root(1, D, 0)
            for j in range(KD):
                sc.wait_ge(h_done, j + 1)
                square(h[:, j, :], 2 * KD + j, j)
            root(2, D, 0)
            for j in range(KD):
                hi(Xh[:, j, :], KD + j, j)
            if not block1_only:
                sc.wait_ge(c_in, 16)
                act_(cact[:, :], cact[:, :], ACT.Silu).then_inc(cact_done, 1)
                sc.wait_ge(ang_done, 1)
                act_(rope_q[:, :], sq[:, 0, :], ACT.Sin).then_inc(rope_done, 1)
            f0, f1 = FILL1[0] - KF, FILL1[1] - KF
            with sc.Fori(0, KF // 2) as i:
                for s in range(2):
                    slot_hi(S_GU + 1 + s + 2 * i, (S_GU + s + 1) // 2 + i, (S_GU + s + 1) % 2)
                    sc.wait_ge(tile_full, tf.val(1 + s) + 2 * i)
                    sc.wait_ge(bank_read[1], f1 - 2 + s + 2 * i)
                    act_(sgate[:, s, :], bank(0), ACT.Silu).then_inc(bank_read[0], 1)
            tf.add(KF)

            def down_hi(q, par):
                if not (isinstance(q, int) and q < 2):
                    sc.wait_ge(slot_done, q + (S_DOWN - 1))
                for kk in range(2):
                    src = act[:, 2 * q + kk, :] if isinstance(q, int) else \
                        act[:, bass.ds(2 * q + kk, 1), :].rearrange("p a n -> p (a n)")
                    act_(act_h[:, 2 * par + kk, :], src, ACT.Copy).then_inc(ah_done, 1)

            sc.wait_ge(bank_read[1], FILL1[1] - 1)
            down_hi(0, 0)
            first_block_hi(S_DOWN + 1)
            down_hi(1, 1)
            with sc.Fori(1, 5) as i:
                for par in range(2):
                    q = 2 * i + par
                    slot_hi(q + S_DOWN, i + (S_DOWN + par) // 2, (S_DOWN + par) % 2)
                    down_hi(q, par)
            first_block_hi(S_DOWN + 10)
            down_hi(10, 0)
            sc.wait_ge(slot_done, SLOTS1)
            if not block1_only:
                sc.wait_ge(ada_done, 2 * KF + 1)
            for j in range(KD):
                square(bank(j), 3 * KD + j, j)
                act_(y[:, j, :], bank(j), ACT.Copy).then_inc(bank_read[j] if j < 2 else down_read, 1)
            root(3, D, 0)
            assert tf.n == TF1, tf.n
            if block1_only:
                return

            with sc.Fori(0, LAYERS) as L:
                G, GH = SLOTS1 + SLOTS2 * L, SLOTS1 // 2 + SLOTS2 // 2 * L
                tf = Tally(TF1 + TF2 * L)
                split0 = SP1 + SP2 * L
                nsum = NORM1 + NORM2 * L
                nadd = SQ1 + SQ2 * L
                b1 = FILL1[1] + FILL2 * L

                def next_hi(s):
                    if s < SLOTS2:
                        slot_hi(G + s, GH + s // 2, s % 2)

                next_hi(0)
                for j in range(KD):
                    hi(Xh[:, j, :], split0 + j, j)
                for k in range(5):
                    if k % 2 == 0:
                        next_hi(k // 2 + 1)
                    full(tf, G + k // 2, k % 2 == 1)
                    square(bank(k % 2), nadd + k, k)
                    act_(lat[:, k, :], bank(k % 2), ACT.Copy).then_inc(bank_read[k % 2], 1)
                root(nsum, 3 * P, 0)
                for j in range(3):
                    hi(lat_h[:, j, :], split0 + (KD + j), KD + j)
                sc.wait_ge(kpe_done, L + 1)
                act_(krope[96:P, 0, :], krope[64:96, 0, :], ACT.Copy).then_inc(kpe_both, 1)
                next_hi(L_CG + 1)
                for j in range(2):
                    full(tf, G + L_CG, j == 1)
                    act_(cg[:, j, :], bank(j), ACT.Silu).then_inc(bank_read[j], 1)
                root(nsum + 1, 2 * P, 0)
                for j in range(3, 5):
                    hi(lat_h[:, j, :], split0 + (KD + j), KD + j)
                next_hi(L_CG + 2)
                for j in range(2):
                    full(tf, G + (L_CG + 1), j == 1)
                    act_(cg[:, 2 + j, :], bank(j), ACT.Silu).then_inc(bank_read[j], 1)
                for s in range(2):
                    next_hi(L_UQ + s + 1)
                    tf.add(3)
                next_hi(L_UKV + 1)
                for j in range(4):
                    full(tf, G + L_UKV, False)
                    for e in range(2):
                        last = act_(K[0:DH, 2 * j + e, :], bank(j % 2, T, DH * e, DH * (e + 1)), ACT.Copy,
                                    scale=-MLA_SCALE)
                    last.then_inc(bank_read[j % 2], 1)
                for t in range(NB):
                    full(tf, G + L_UKV, t == NB - 1)
                    act_(Vc[:, t, :], bank(t % 2), ACT.Copy).then_inc(bank_read[t % 2], 1)

                U0 = NB * HEADS * L

                def a_tile(i, j):
                    if i >= 6:
                        return
                    if i >= 4:
                        full(tf, G + (L_A + i), j == 1)
                        act_(ag[:, 2 * (i - 4) + j, :], bank(j), ACT.Silu).then_inc(bank_read[j], 1)
                    elif j == 0:
                        full(tf, G + (L_A + i), False)
                        if i:
                            sc.wait_ge(bank_read[1], b1 + (13 + i))
                        act_(sig[:, :], bank(0), ACT.Sigmoid).then_inc(bank_read[0], 1)

                for hd in range(HEADS):
                    if hd < 6:
                        next_hi(L_A + hd + 1)
                    for b in range(NB):
                        n = P * (b + 1)
                        sc.wait_ge(max2_done, U0 + (NB * hd + b + 1))
                        act_(Pc[:, P * tri(b):P * tri(b) + n], bank(2 + b, n), ACT.Exp, scale=-1.0,
                             bias=nmax[:, b:b + 1], accum_out=rsum[:, b:b + 1]).then_inc(exp2_done, 1)
                    a_tile(hd, 0)
                    for b in range(NB):
                        sc.wait_ge(t2_full, U0 + (NB * hd + b + 1))
                        if b == 0 and hd:
                            sc.wait_ge(pv2_done, HEADS * L + hd)
                        act_(PTc[:, P * tri(b):P * tri(b + 1)], bank(2 + b, P * (b + 1)), ACT.Copy
                             ).then_inc(pt2_done, 1)
                    a_tile(hd, 1)
                    if hd and hd % 2 == 0:
                        i = hd // 2 - 1
                        hi(yc_h[:, i, :], split0 + (KD + 5 + i), KD + 5 + i)
                hi(yc_h[:, 3, :], split0 + (KD + 8), KD + 8)
                for s in range(8):
                    next_hi(L_B + s + 1)
                    full(tf, G + (L_B + s), False)
                    sc.wait_ge(bank_read[1], b1 + (L_BANK1 + s - 1))
                    act_(btmp[:, s % 2, :], bank(0), ACT.Copy if s < 4 else ACT.Silu).then_inc(bank_read[0], 1)
                    if s >= 5:
                        hi(yb_h[:, s - 5, :], split0 + (KD + 9 + s - 5), KD + 9 + s - 5)
                hi(yb_h[:, 3, :], split0 + (KD + 12), KD + 12)
                for j in range(KD):
                    act_(h[:, j, :], h[:, j, :], ACT.Copy, scale=DEEPNORM_ALPHA).then_inc(h_scaled, 1)

                def gates(s, dst, q0):
                    next_hi(s + 1)
                    for j in range(2):
                        full(tf, G + s, j == 1)
                        act_(dst[:, q0 + j, :], bank(j), ACT.Sigmoid).then_inc(bank_read[j], 1)

                for br in range(2):
                    for half in range(2):
                        s = L_M + 6 * br + 3 * half
                        gates(s, gt, 0)
                        gates(s + 1, gt, 2)
                        next_hi(s + 3)
                        tf.add(3)
                for s in range(4):
                    gates(L_M + 12 + s, gt if s < 2 else gt2, 2 * (s % 2))
                    if s == 0:
                        mean(nsum + 2, CA)
                        for t in range(KC):
                            sc.wait_ge(zc_ready, (KC + KD) * L + (t + 1))
                            square(cacc[:, t, :], nadd + (5 + KC + t), t)
                    if s == 1:
                        root(nsum + 3, CA, 1)
                        for t in range(KC):
                            sc.wait_ge(ln_mid, (KC + KD) * L + (t + 1))
                            act_(cacc[:, t, :], cacc[:, t, :], ACT.Silu, scale=vec(L, V_LAG + t),
                                 bias=vec(L, V_LAB + t)).then_inc(ya_act, 1)
                        for t in range(KC):
                            hi(ya_h[:, t, :], split0 + (KD + 13 + t), KD + 13 + t)
                for s in range(2):
                    next_hi(L_M + 17 + s)
                    tf.add(3)
                    for j in range(4 * s, 4 * s + 4):
                        sc.wait_ge(t_ready, split0 + (KD + 17 + j + 1))
                        act_(Xh[:, j, :], m[:, j, :], ACT.Copy).then_inc(hi_done, 1)
                for s in range(4):
                    next_hi(L_WO + s + 1)
                    tf.add(1)
                mean(nsum + 4, D)
                for j in range(KD):
                    sc.wait_ge(zc_ready, (KC + KD) * L + (KC + j + 1))
                    square(h[:, j, :], nadd + (5 + 2 * KC + KD + j), j)
                root(nsum + 5, D, 1)
                for j in range(KD):
                    sc.wait_ge(ln_mid, (KC + KD) * L + (KC + j + 1))
                    act_(h[:, j, :], h[:, j, :], ACT.Identity, scale=vec(L, V_LG + j), bias=vec(L, V_LB + j)
                         ).then_inc(ln_out, 1)
                assert tf.n == TF2, tf.n

        @block.vector
        def _(ve):
            own = Chain(ve, dve_own)

            def tt(o_, a_, b_, op):
                return nc.vector.tensor_tensor(o_, a_, b_, op)

            def ts(o_, a_, s1, s2, op0, op1=None):
                return nc.vector.tensor_scalar(o_, a_, s1, s2, op0, op1) if op1 is not None else \
                    nc.vector.tensor_scalar(o_, a_, s1, s2, op0)

            def stt(o_, a_, s_, b_, op0, op1):
                return nc.vector.scalar_tensor_tensor(o_, a_, s_, b_, op0, op1)

            def slot_lo(g, par):
                ve.wait_ge(w_hi_done, g + 1)
                tt(w_lo[:, par, :], w_raw[:, par, :], w_hi[:, par, :], ALU.subtract).then_inc(w_lo_done, 1)

            def rest(n, k, xh, xl, src=None):
                ve.wait_ge(hi_done, n + 1)
                tt(xl, tmp[:, k % 2, :] if src is None else src, xh, ALU.subtract).then_inc(lo_done, 1)

            def split(items, n0, k0):
                for i, (pre, _, _) in enumerate(items):
                    if not (isinstance(n0, int) and n0 + i < 2):
                        ve.wait_ge(lo_done, n0 + (i - 1))
                    pre(tmp[:, (k0 + i) % 2, :]).then_inc(t_ready, 1)
                    if i:
                        rest(n0 + (i - 1), k0 + i - 1, items[i - 1][1], items[i - 1][2])
                rest(n0 + (len(items) - 1), k0 + len(items) - 1, items[-1][1], items[-1][2])

            def inv_root(norm):
                ve.wait_ge(rt_done, norm + 1)
                own.link(nc.vector.reciprocal(R[:, :], R[:, :]))

            def full(tf, g, last):
                if last:
                    ve.wait_ge(slot_done, g + 1)
                else:
                    tf.add()
                    ve.wait_ge(tile_full, tf.val())

            tf = Tally()
            nc.vector.memset(eps[:, 0:1], 1e-6)
            nc.vector.memset(eps[:, 1:2], 1e-5)
            nc.vector.memset(fx[:, NB, :], 0.0)
            nc.vector.memset(Qb[64:66, :, :], 1.0)
            nc.vector.memset(Kb[64:66, :, :], 1.0)
            nc.vector.memset(ones[:, :], 1.0).then_inc(init_done, 1)
            ve.wait_ge(init_done, 1)
            ve.wait_ge(consts_in, 16 * N_CONST)
            for hd in range(HEADS):
                last = ts(tabb[:, hd, :], ones[0:33, :], tab[:, hd:hd + 1], -1.0, ALU.mult, ALU.mult)
            last.then_inc(tabb_done, 1)
            ts(nsink[:, :], sinkb[:, :], -1.0, None, ALU.mult).then_inc(nsink_done, 1)
            ve.wait_ge(meta_sq, 1)
            nc.vector.tensor_reduce(accm[:, :], sqm[:, :, :].rearrange("p k t -> p t k"), AX.X, ALU.add
                                    ).then_inc(meta_sum, 1)
            ve.wait_ge(wf_ready, 1)
            tt(wf_lo[:, :, :], wf[:, :, :], wf_hi[:, :, :], ALU.subtract).then_inc(wf_split, 1)
            slot_lo(0, 0)
            inv_root(0)
            split([((lambda o_, j=j: stt(o_, h[:, j, :], vec1[:, j:j + 1], R[:, :], ALU.mult, ALU.mult)),
                    Xh[:, j, :], Xl[:, j, :]) for j in range(KD)], 0, 0)
            ve.wait_ge(meta_rt, 1)
            own.link(nc.vector.reciprocal(Rm[:, :], Rm[:, :]))
            for j in range(KD):
                stt(meta_n[:, j, :], metaT[:, j, :], vec1[:, j:j + 1], Rm[:, :], ALU.mult, ALU.mult
                    ).then_inc(meta_norm, 1)
            ve.wait_ge(meta_hi, 1)
            tt(Ml[:, :, :], meta_n[:, :, :], Mh[:, :, :], ALU.subtract).then_inc(meta_lo, 1)
            slot_lo(1, 1)

            def v_read(g, c0, n, first_bank):
                for t in range(NB):
                    full(tf, g, t == NB - 1)
                    b = (first_bank + t) % 2
                    if t == NB - 1:
                        nc.vector.tensor_copy(Vm[0:NM, c0:c0 + n], bank(3, n, 0, NM))
                    nc.vector.tensor_copy(V[:, t, c0:c0 + n], bank(b, n)).then_inc(bank_read[b], 1)

            tf.add(1)
            v_read(0, 0, P, 1)
            slot_lo(2, 0)
            ve.wait_ge(f_full, 1)
            for t in range(NB):
                last = tt(fx[:, t, :], bank(B_O, 8, c0=32 + 8 * t), bfb[:, :], ALU.add)
            last.then_inc(f_biased, 1)
            tt(fx[0:NM, NB, :], bank(B_O, 8, 0, NM, c0=32 + 8 * NB), bfb[0:NM, :], ALU.add).then_inc(f_biased, 1)
            tf.add(1)
            slot_lo(3, 1)
            ve.wait_ge(f_log, 1)
            stt(ls[:, :, :], fx[:, :, :], 0.0, fa[:, :, :], ALU.min, ALU.subtract).then_inc(ls_done, 1)
            tf.add(1)
            ve.wait_ge(cum_full, 1)
            nc.vector.tensor_copy(cum[:, 0:NM], bank(B_O, NM, 0, 8))
            own.link(nc.vector.tensor_copy(cum[:, NM:NM + T], bank(B_ST, T, 0, 8)))
            ts(ncum[:, 0:NM], cum[:, 0:NM], -1.0, None, ALU.mult).then_inc(cum_done, 1)
            ts(ncum[:, NM:NM + T], cum[:, NM:NM + T], -1.0, None, ALU.mult).then_inc(cum_done, 1)
            for s in (3, 4):
                slot_lo(s + 1, (s + 1) % 2)
                v_read(s, P + 2 * P * (s - 3), 2 * P, 0)
            for s in range(5, 9):
                slot_lo(s + 1, (s + 1) % 2)
                tf.add(1)

            def max_unit(u):
                b, k = u % NB, u % 4
                if u < UNITS // 2:
                    n, first = NM + P * (b + 1), 3e38
                    add = mask[:, 384 - P * b:384 - P * b + n]
                else:
                    i = (u - UNITS // 2) // NB
                    hs = i // 2 + 4 * (i % 2)
                    n = NM + P * (min(b, 1) + 1)
                    add = (bias1 if b else bias0)[:, hs, :]
                    first = nsink[:, hs:hs + 1]
                c0 = 2 * (u % 3) * T + T - NM
                ve.wait_ge(s_full, u + 1)
                nc.vector.tensor_tensor_reduce(ps[:, c0:c0 + n], ps[:, c0:c0 + n], add, 1.0, first, ALU.add, ALU.min,
                                               nmax[:, k:k + 1]).then_inc(max_done, 1)

            def norm_unit(u):
                b, k = u % NB, u % 4
                swa = u >= UNITS // 2
                n = NM + P * ((min(b, 1) if swa else b) + 1)
                ve.wait_ge(exp_done, UNITS // 2 + 2 * (u + 1 - UNITS // 2) if swa else u + 1)
                if swa:
                    own.link(tt(rsum[:, k:k + 1], rsum[:, k:k + 1], esink[:, k:k + 1], ALU.add))
                own.link(nc.vector.reciprocal(rinv[:, k:k + 1], rsum[:, k:k + 1]))
                ts(Pr[:, u % 3, 0:n], Pr[:, u % 3, 0:n], rinv[:, k:k + 1], None, ALU.mult).then_inc(p_done, 1)

            def out_lo(i):
                ve.wait_ge(o_hi, i + 1)
                tt(Xl[:, (4 + i) % 8, :], bank(B_O), Xh[:, (4 + i) % 8, :], ALU.subtract).then_inc(o_lo, 1)

            max_unit(0)
            max_unit(1)
            for u in range(UNITS):
                norm_unit(u)
                if u + 2 == UNITS // 2:
                    ve.wait_ge(bias_in, 64)
                    ve.wait_ge(nsink_done, 1)
                if u + 2 < UNITS:
                    max_unit(u + 2)
                if u % (2 * NB) == 1 and u > 1:
                    out_lo(u // (2 * NB) - 1)
            out_lo(7)

            for s in range(S_OUT, S_GU):
                slot_lo(s + 1, (s + 1) % 2)
                tf.add(1)

            def add_norm(norm, g0):
                inv_root(norm)
                for j in range(KD):
                    own.link(stt(tmp[:, j % 2, :], y[:, j, :], vec1[:, g0 + j:g0 + j + 1], R[:, :],
                                 ALU.mult, ALU.mult))
                    tt(h[:, j, :], h[:, j, :], tmp[:, j % 2, :], ALU.add).then_inc(h_done, 1)

            add_norm(1, KD)
            inv_root(2)
            split([((lambda o_, j=j: stt(o_, h[:, j, :], vec1[:, 2 * KD + j:2 * KD + j + 1], R[:, :],
                                         ALU.mult, ALU.mult)),
                    Xh[:, j, :], Xl[:, j, :]) for j in range(KD)], KD, 0)

            if not block1_only:
                ang, cnt = sq[:, 0, :], sq[:, 1, :]
                ve.wait_ge(pos_in, 16)
                own.link(nc.vector.tensor_copy(posf[:, :], pos[:, :]))
                own.link(ts(ang, posf[:, :], ropec[:, 0:1], None, ALU.mult))
                own.link(ts(cnt, ang, 1.0 / (2 * math.pi), ropec[:, 1:2], ALU.mult, ALU.add))
                own.link(ts(cnt, cnt, ROUND, None, ALU.add))
                own.link(ts(cnt, cnt, -ROUND, None, ALU.add))
                for part in (TWO_PI_1, TWO_PI_2, TWO_PI_3):
                    own.link(stt(ang, cnt, -part, ang, ALU.mult, ALU.add))
                own.link(ts(ang, ang, ropec[:, 2:3], 3.1415925, ALU.add, ALU.min))
                ts(ang, ang, -3.1415925, None, ALU.max).then_inc(ang_done, 1)
                ve.wait_ge(rope_done, 1)
                own.link(ts(rope_q[:, :], rope_q[:, :], ropec[:, 3:4], None, ALU.mult))
                nc.vector.memset(rope_q[0:DH, :], 1.0).then_inc(ada_done, 1)
                ve.wait_ge(cact_done, 1)

            def ada_column(t, half, par, prod):
                ve.wait_ge(adaw_in[par], 16 * half + 16)
                ve.wait_ge(ada_done, t + 1)
                nc.vector.tensor_tensor_reduce(prod, ada_w[:, par, :], cact[:, :], 1.0, 0.0, ALU.mult, ALU.add,
                                               ada_sum[:, par:par + 1]).then_inc(ada_done, 1)
                ve.wait_ge(ada_done, t + 2)
                nc.vector.tensor_copy(ada[:, t:t + 1] if isinstance(t, int) else ada[:, bass.ds(t, 1)],
                                      ada_sum[:, par:par + 1]).then_inc(ada_copied, 1)

            f0, f1 = FILL1[0] - KF, FILL1[1] - KF
            with ve.Fori(0, KF // 2) as i:
                for s in range(2):
                    slot_lo(S_GU + 1 + s + 2 * i, (S_GU + s + 1) % 2)
                    ve.wait_ge(bank_read[0], f0 + s + 2 * i)
                    ve.wait_ge(slot_done, S_GU + 1 + s + 2 * i)
                    tt(act[:, bass.ds(s + 2 * i, 1), :].rearrange("p a n -> p (a n)"), sgate[:, s, :], bank(1), ALU.mult
                       ).then_inc(bank_read[1], 1)
                    if not block1_only:
                        for par in range(2):
                            ada_column(4 * i + (2 * s + par), 2 * i + s, par, ada_prod[:, :])
            tf.add(KF)

            def down_lo(q, par):
                for kk in range(2):
                    ve.wait_ge(ah_done, 2 * q + kk + 1)
                    src = act[:, 2 * q + kk, :] if isinstance(q, int) else \
                        act[:, bass.ds(2 * q + kk, 1), :].rearrange("p a n -> p (a n)")
                    tt(act_l[:, 2 * par + kk, :], src, act_h[:, 2 * par + kk, :], ALU.subtract).then_inc(al_done, 1)

            down_lo(0, 0)
            slot_lo(S_DOWN + 1, (S_DOWN + 1) % 2)
            down_lo(1, 1)
            with ve.Fori(1, 5) as i:
                for par in range(2):
                    q = 2 * i + par
                    slot_lo(q + S_DOWN, (S_DOWN + par) % 2)
                    down_lo(q, par)
            slot_lo(S_DOWN + 10, (S_DOWN + 10) % 2)
            down_lo(10, 0)
            if not block1_only:
                for t in range(2 * KF, 24 * LAYERS):
                    ada_column(t, t // 2, t % 2, sgate[:, :, :].rearrange("p a n -> p (a n)"))
                ve.wait_ge(ada_copied, 24 * LAYERS)
                for l in range(LAYERS):
                    own.link(tt(ada[:, 24 * l:24 * l + 24], ada[:, 24 * l:24 * l + 24], vec2[:, l, V_BADA:V_BADA + 24],
                                ALU.add))
                    own.link(ts(ada[:, 24 * l + 8:24 * l + 16], ada[:, 24 * l + 8:24 * l + 16], 1.0, None, ALU.add))
            add_norm(3, 3 * KD)
            if block1_only:
                return
            assert own.n == OWN1, own.n
            assert tf.n == TF1, tf.n

            with ve.Fori(0, LAYERS) as L:
                own = Chain(ve, dve_own, OWN1 + OWN2 * L)
                tf = Tally(TF1 + TF2 * L)
                G = SLOTS1 + SLOTS2 * L
                split0 = SP1 + SP2 * L
                nsum = NORM1 + NORM2 * L
                bf = Fills(FILL1[0] + FILL2 * L, FILL1[1] + FILL2 * L)

                def next_lo(s):
                    if s < SLOTS2:
                        slot_lo(G + s, s % 2)

                def ada_col(c):
                    return ada[:, bass.ds(24 * L + c, 1)]

                next_lo(0)
                ve.wait_ge(h_done, 2 * KD)
                split([((lambda o_, j=j: ts(o_, h[:, j, :], ada_col(8 + j), ada_col(j), ALU.mult, ALU.add)),
                        Xh[:, j, :], Xl[:, j, :]) for j in range(KD)], split0, 0)
                for s in range(3):
                    next_lo(s + 1)
                tf.add(3)
                ve.wait_ge(slot_done, G + 3)
                tt(krope[64:96, 0, :], bank(1, T, 64, 96), rope_q[64:96, :], ALU.mult)
                tt(krope[64:96, 1, :], bank(1, T, 96, P), rope_q[96:P, :], ALU.mult).then_inc(bank_read[1], 1)
                bf.f[0].add(3)
                bf.f[1].add(3)
                ve.wait_ge(bank_read[1], bf.f[1].val())
                own.link(tt(krope[64:96, 0, :], krope[64:96, 0, :], krope[64:96, 1, :], ALU.add))
                ts(krope[64:96, 0, :], krope[64:96, 0, :], -MLA_SCALE, None, ALU.mult).then_inc(kpe_done, 1)

                def latents(norm, j0, j1, g0):
                    inv_root(norm)
                    split([((lambda o_, j=j: stt(o_, lat[:, j, :], vec(L, g0 + j - j0), R[:, :], ALU.mult, ALU.mult)),
                            lat_h[:, j, :], lat_l[:, j, :]) for j in range(j0, j1)], split0 + (KD + j0), KD + j0)

                latents(nsum, 0, 3, V_QG)
                next_lo(L_CG + 1)
                latents(nsum + 1, 3, 5, V_KG)
                next_lo(L_CG + 2)
                tf.add(2)
                bf.f[0].add(2)
                bf.f[1].add(2)
                for s in range(2):
                    next_lo(L_UQ + s + 1)
                    for j in range(4):
                        full(tf, G + (L_UQ + s), j == 3)
                        tt(Q[:, 4 * s + j, :], bank(j % 2), rope_q[:, :], ALU.mult).then_inc(bank_read[j % 2], 1)
                        bf.take(j % 2)
                next_lo(L_UKV + 1)
                tf.add(7)
                bf.f[0].add(4)
                bf.f[1].add(4)

                U0 = NB * HEADS * L
                nc.vector.memset(ain[:, :, 0:TAPS - 1], 0.0)

                def max2(hd, b):
                    n = P * (b + 1)
                    ve.wait_ge(consts_in, 16 * N_CONST)
                    ve.wait_ge(s2_full, U0 + (NB * hd + b + 1))
                    ve.sem_inc(scores_seen, 1)
                    nc.vector.tensor_tensor_reduce(bank(2 + b, n), bank(2 + b, n), mask[:, NM + 384 - P * b:NM + 384 + P],
                                                   1.0, 3e38, ALU.add, ALU.min, nmax[:, b:b + 1]).then_inc(max2_done, 1)

                def norm2(hd, b):
                    p = Pc[:, P * tri(b):P * tri(b + 1)]
                    ve.wait_ge(exp2_done, U0 + (NB * hd + b + 1))
                    own.link(nc.vector.reciprocal(rinv[:, b:b + 1], rsum[:, b:b + 1]))
                    ts(p, p, rinv[:, b:b + 1], None, ALU.mult).then_inc(p2_done, 1)

                def gate_c(i):
                    ve.wait_ge(pv2_done, HEADS * L + 2 * (i + 1))
                    split([((lambda o_: tt(o_, bank(B_O), cg[:, i, :], ALU.mult)), yc_h[:, i, :], yc_l[:, i, :])],
                          split0 + (KD + 5 + i), KD + 5 + i)

                for hd in range(HEADS):
                    if hd < 6:
                        next_lo(L_A + hd + 1)
                    max2(hd, 0)
                    for b in range(NB):
                        if b + 1 < NB:
                            max2(hd, b + 1)
                        norm2(hd, b)
                    if hd < 4:
                        tf.add(1)
                        ve.wait_ge(slot_done, G + (L_A + hd + 1))
                        bf.take(1)
                        ve.wait_ge(bank_read[0], bf.take(0))
                        tt(ain[:, hd, TAPS - 1:TAPS - 1 + T], sig[:, :], bank(1), ALU.mult).then_inc(bank_read[1], 1)
                    elif hd < 6:
                        tf.add(1)
                        bf.take(0)
                        bf.take(1)
                    if hd and hd % 2 == 0:
                        gate_c(hd // 2 - 1)
                gate_c(3)

                def conv_step(n):
                    t, part = n // 5, n % 5
                    k0, k1 = (7 * part - max(part - 1, 0)), 7 * (part + 1) - part
                    for k in range(k0, k1):
                        src = ain[:, t, k:k + T]
                        if k == 0:
                            ins = ts(cacc[:, t, :], src, vec(L, V_CAW + TAPS * t), vec(L, V_CAB + t), ALU.mult, ALU.add)
                        else:
                            ins = stt(cacc[:, t, :], src, vec(L, V_CAW + TAPS * t + k), cacc[:, t, :],
                                      ALU.mult, ALU.add)
                        if k == TAPS - 1:
                            ins.then_inc(conv_done, 1)
                        else:
                            own.link(ins)

                nc.vector.memset(bx[:, :, 0:CB - 1], 0.0)
                for s in range(8):
                    next_lo(L_B + s + 1)
                    tf.add(1)
                    bf.take(1)
                    ve.wait_ge(bank_read[0], bf.take(0))
                    ve.wait_ge(slot_done, G + (L_B + s + 1))
                    if s < 4:
                        tt(bx[:, s, CB - 1:CB - 1 + T], btmp[:, s % 2, :], bank(1), ALU.mult).then_inc(bank_read[1], 1)
                    else:
                        i, c, gb = s - 4, btmp[:, 2, :], btmp[:, 3, :]
                        tt(gb, btmp[:, s % 2, :], bank(1), ALU.mult).then_inc(bank_read[1], 1)
                        if i == 0:
                            ve.wait_ge(bank_read[1], bf.f[1].val())
                        own.link(ts(c, bx[:, i, 0:T], vec(L, V_CBW + CB * i), None, ALU.mult))
                        for k in range(1, CB):
                            own.link(stt(c, bx[:, i, k:k + T], vec(L, V_CBW + CB * i + k), c, ALU.mult, ALU.add))
                        ve.wait_ge(lo_done, split0 + (KD + 8 + i))
                        tt(tmp[:, (KD + 9 + i) % 2, :], c, gb, ALU.mult).then_inc(t_ready, 1)
                        if i:
                            rest(split0 + (KD + 8 + i), KD + 8 + i, yb_h[:, i - 1, :], yb_l[:, i - 1, :])
                    conv_step(s)
                rest(split0 + (KD + 12), KD + 12, yb_h[:, 3, :], yb_l[:, 3, :])

                def merge_tiles(s, half, g_, br):
                    sums_at = []
                    for j in range(4):
                        full(tf, G + s, j == 3)
                        mj = m[:, 4 * half + j, :]
                        bf.take(j % 2)
                        if br == 1 and j >= 2:
                            own.need(sums_at[j - 2])
                        if br == 2 and j >= 2:
                            ve.wait_ge(t_ready, split0 + (KD + 17 + 4 * half + j - 1))
                        if br == 0:
                            tt(mj, g_[:, j, :], bank(j % 2), ALU.mult).then_inc(bank_read[j % 2], 1)
                        else:
                            tt(tmp[:, j % 2, :], g_[:, j, :], bank(j % 2), ALU.mult).then_inc(bank_read[j % 2], 1)
                            ve.wait_ge(bank_read[j % 2], bf.f[j % 2].val())
                            ins = tt(mj, mj, tmp[:, j % 2, :], ALU.add)
                            if br == 2:
                                ins.then_inc(t_ready, 1)
                                if 4 * half + j:
                                    m_rest(4 * half + j - 1)
                            else:
                                sums_at.append(own.mark(ins))

                def m_rest(j):
                    rest(split0 + (KD + 17 + j), 0, Xh[:, j, :], Xl[:, j, :], src=m[:, j, :])

                for br in range(2):
                    for half in range(2):
                        s = L_M + 6 * br + 3 * half
                        for e in range(2):
                            next_lo(s + e + 1)
                            conv_step(8 + 6 * br + 3 * half + e)
                            tf.add(1)
                            bf.take(0)
                            bf.take(1)
                        next_lo(s + 3)
                        conv_step(8 + 6 * br + 3 * half + 2)
                        merge_tiles(s + 2, half, gt, br)
                for s in range(4):
                    next_lo(L_M + 13 + s)
                    tf.add(1)
                    bf.take(0)
                    bf.take(1)
                    if s == 0:
                        ve.wait_ge(rt_done, nsum + 3)
                        for t in range(KC):
                            tt(cacc[:, t, :], cacc[:, t, :], R[:, :], ALU.subtract).then_inc(zc_ready, 1)
                    if s == 1:
                        inv_root(nsum + 3)
                        for t in range(KC):
                            tt(cacc[:, t, :], cacc[:, t, :], R[:, :], ALU.mult).then_inc(ln_mid, 1)

                        def gated(o_, t):
                            ve.wait_ge(ya_act, KC * L + (t + 1))
                            return tt(o_, cacc[:, t, :], ag[:, t, :], ALU.mult)

                        split([((lambda o_, t=t: gated(o_, t)), ya_h[:, t, :], ya_l[:, t, :]) for t in range(KC)],
                              split0 + (KD + 13), KD + 13)
                for half in range(2):
                    next_lo(L_M + 17 + half)
                    merge_tiles(L_M + 16 + half, half, (gt, gt2)[half], 2)
                m_rest(KD - 1)

                for s in range(4):
                    next_lo(L_WO + s + 1)
                    for j in range(2):
                        full(tf, G + (L_WO + s), j == 1)
                        jj = 2 * s + j
                        ve.wait_ge(h_scaled, KD * L + (jj + 1))
                        stt(h[:, jj, :], bank(j), ada_col(16 + jj), h[:, jj, :], ALU.mult, ALU.add
                            ).then_inc(bank_read[j], 1)
                        bf.take(j)
                ve.wait_ge(rt_done, nsum + 5)
                for j in range(KD):
                    tt(h[:, j, :], h[:, j, :], R[:, :], ALU.subtract).then_inc(zc_ready, 1)
                inv_root(nsum + 5)
                for j in range(KD):
                    tt(h[:, j, :], h[:, j, :], R[:, :], ALU.mult).then_inc(ln_mid, 1)
                ve.wait_ge(ln_out, KD * L + KD)
                assert own.n == OWN2, own.n
                assert tf.n == TF2, tf.n
                assert bf.f[0].n == FILL2 and bf.f[1].n == FILL2, (bf.f[0].n, bf.f[1].n)


def _constants():
    f = np.float32
    p = np.arange(P)
    q, k = p[:, None], p[None, :]
    c = {"ident": np.eye(P, dtype=f)}
    c["mask"] = np.concatenate([np.zeros((P, NM + 384), f), np.where(k > q, f(BIG), f(0))], 1)
    c["cum_tri"] = (q <= np.arange(NM + T)[None, :]).astype(f)
    c["outside"] = np.full((1, 8), -BIG, f)
    n = np.arange(0, 272)
    large = 16 + (np.log(np.maximum(n, 1).astype(f) / f(16)) / f(math.log(8)) * f(16)).astype(np.int32)
    bucket = np.where(n < 16, n, np.minimum(large, 31))
    onehot = np.zeros((33, ROW), f)
    for j in range(ROW_W):
        d = 255 - j
        onehot[bucket[d] if 0 <= d < 128 else 32, j] = 1
    for j in range(ROW_M):
        onehot[bucket[271 - j], ROW_W + j] = 1
    c["onehot"] = onehot
    rope = np.zeros((P, 4), f)
    freq = (10000.0 ** (-np.arange(0, 32, 2) / 32)).astype(f)
    rope[64:, 0] = np.tile(freq, 4)
    rope[64:96, 1], rope[64:96, 2] = 0.25, math.pi / 2
    rope[:, 3] = 1
    rope[96:112, 3] = -1
    c["ropec"] = rope
    return c


def _tile(w, cols):
    return np.ascontiguousarray(w[:, cols]).reshape(-1, P, len(cols)).transpose(1, 0, 2)


def _slot(*parts):
    flat = [np.concatenate(tiles, axis=2).reshape(P, -1) for tiles in parts]
    flat = np.concatenate(flat, axis=1)
    return np.pad(flat, ((0, 0), (0, SLOT - flat.shape[1])))


def _stream(x):
    r = lambda a, n=P: np.arange(a, a + n)
    w_in, w_out, w_gu, w_down = (np.asarray(x[k])[0] for k in ("w_in", "w_out", "w_gate_up", "w_down"))
    slots = []

    def pair(w, a, b):
        slots.append(_slot([_tile(w, a), _tile(w, b)]))

    qa, ka, va, qb, kb, vb = 0, 512, 640, 768, 1280, 1792
    pair(w_in, r(ka), r(va))
    for c in (kb, vb, qb):
        for i in range(2):
            pair(w_in, r(c + 256 * i), r(c + 256 * i + 128))
    heads = [np.concatenate([r(DH * i, DH), r(DH * (4 + i), DH)]) for i in range(4)]
    pair(w_in, qa + heads[0], qa + heads[1])
    pair(w_in, qa + heads[2], qa + heads[3])
    rows = np.concatenate(heads + [r(512, 512)])
    for i in range(4):
        pair(w_out[rows], r(256 * i), r(256 * i + 128))
    for t in range(KF):
        pair(w_gu, r(P * t), r(FF + P * t))
    for i in range(KF // 2):
        slots.append(w_down[256 * i:256 * i + 256].reshape(2, P, D).transpose(1, 0, 2).reshape(P, -1))
    assert len(slots) == SLOTS1
    for l in range(LAYERS):
        w = np.asarray(x["w_in_2"])[l]
        a1, a2, agc, xb, gb, gc, bg, ql, kl, kr, cgc, ml = \
            0, 512, 1024, 1536, 2048, 2560, 3072, 3584, 3968, 4224, 4256, 4768
        pe, sw = r(kr, 32), np.concatenate([r(kr + 16, 16), r(kr, 16)])
        pair(w, r(ql), r(ql + 128))
        pair(w, r(ql + 256), r(kl))
        pair(w, r(kl + 128), np.concatenate([pe, sw, pe, sw]))
        for i in range(2):
            pair(w, r(cgc + 256 * i), r(cgc + 256 * i + 128))
        uq, ukv = np.asarray(x["w_uq_2"])[l], np.asarray(x["w_ukv_2"])[l]
        for i in range(2):
            tiles = []
            for hd in range(4 * i, 4 * i + 4):
                c = 96 * hd
                tiles.append(_tile(uq, np.concatenate([r(c, 96), r(c + 80, 16), r(c + 64, 16)])))
            slots.append(_slot(tiles))
        nope = [_tile(ukv, np.concatenate([r(256 * i, DH), r(256 * i + 128, DH)])) for i in range(4)]
        v = _tile(ukv, np.concatenate([r(128 * hd + DH, DH) for hd in range(8)]))
        slots.append(_slot(nope, [v]))
        for i in range(4):
            pair(w, r(a2 + P * i), r(a1 + P * i))
        for i in range(2):
            pair(w, r(agc + 256 * i), r(agc + 256 * i + 128))
        for i in range(4):
            pair(w, r(xb + P * i), r(gc + P * i))
        for i in range(4):
            pair(w, r(bg + P * i), r(gb + P * i))

        def g_slot(br, i):
            pair(w, r(ml + D * br + 256 * i), r(ml + D * br + 256 * i + 128))

        def y_slot(name, half):
            slots.append(_slot([_tile(np.asarray(x[name])[l], r(512 * half, 512))]))

        for br, name in ((2, "w_c_out_2"), (1, "w_b_out_2")):
            for half in range(2):
                g_slot(br, 2 * half)
                g_slot(br, 2 * half + 1)
                y_slot(name, half)
        for i in range(4):
            g_slot(0, i)
        for half in range(2):
            y_slot("w_a_out_2", half)
        for i in range(4):
            pair(np.asarray(x["w_o_2"])[l], r(256 * i), r(256 * i + 128))
    assert len(slots) == N_SLOTS
    return np.stack(slots)


def _columns(v):
    return np.asarray(v).reshape(-1, P).T


def kernel(**inputs):
    import concourse.bacc as bacc
    from concourse.bass_utils import run_bass_kernel_spmd

    x = {k: np.asarray(v) for k, v in inputs.items()}
    arrays = dict(_constants())
    arrays["xT"] = x["x"][0].T.reshape(KD, P, T).transpose(1, 0, 2)
    arrays["metaT"] = x["meta_tokens"].T.reshape(KD, P, NM).transpose(1, 0, 2)
    arrays["w"] = _stream(x)
    arrays["wf"] = _tile(x["w_in"][0], np.arange(2304, 2312))
    arrays["vec1"] = np.concatenate([_columns(x[k][0]) for k in
                                     ("ln_pre_mix", "ln_post_mix", "ln_pre_ffn", "ln_post_ffn")], 1)
    vecs = []
    for l in range(LAYERS):
        caw = x["conv_a_w_2"][l].reshape(TAPS, KC, P).transpose(2, 1, 0).reshape(P, -1)
        cbw = x["conv_b_w_2"][l].reshape(CB, KC, P).transpose(2, 1, 0).reshape(P, -1)
        vecs.append(np.concatenate([_columns(x["b_ada_2"][l]), caw, _columns(x["conv_a_b_2"][l]),
                                    _columns(x["ln_a_g_2"][l]), _columns(x["ln_a_b_2"][l]), cbw,
                                    _columns(x["q_norm_g_2"][l]), _columns(x["kv_norm_g_2"][l]),
                                    _columns(x["ln_g_2"][l]), _columns(x["ln_b_2"][l])], 1))
    arrays["vec2"] = np.stack(vecs, 1)
    arrays["w_ada"] = x["w_ada_2"].transpose(0, 2, 1).reshape(LAYERS * 24, P, D)
    arrays["c"] = x["c_2"][0]
    arrays["positions"] = x["positions_2"][0]
    arrays["rel_bias"] = x["rel_bias"]
    arrays["b_forget"] = x["b_forget"][0]
    arrays["sinks"] = x["sinks"][0]
    arrays = {k: np.ascontiguousarray(v) for k, v in arrays.items()}

    nc = bacc.Bacc("TRN2", target_bir_lowering=False, num_devices=1)
    a = {k: nc.dram_tensor(f"in_{k}", v.shape, mybir.dt.from_np(v.dtype), kind="ExternalInput").ap()
         for k, v in arrays.items()}
    out = nc.dram_tensor("out_0", (P, KD, T), F32, kind="ExternalOutput").ap()
    program(nc, a, out)
    r = run_bass_kernel_spmd(nc, [{f"in_{k}": v for k, v in arrays.items()}], core_ids=[0])
    got = np.asarray(r.results[0]["out_0"])
    return np.ascontiguousarray(got.transpose(1, 0, 2).reshape(D, T).T)[None]
```
